# Optimizing a Trainium2 kernel written in Bass

```python
import math
import jax, jax.numpy as jnp
from jax import lax
import numpy as np

D_MODEL = 1024
BATCH = 1
SEQ = 512
DEPTH = 2

D_MIX = D_MODEL
SSD_HEADS = 8
SSD_HEAD_DIM = 64
SSD_WIDTH = SSD_HEADS * SSD_HEAD_DIM
SSD_GROUPS = 2
SSD_STATE = 128
SSD_CONV = 4
SSD_CHUNK = 128
SSD_CONV_DIM = SSD_WIDTH + 2 * SSD_GROUPS * SSD_STATE
MLA_HEADS = 4
MLA_Q_LORA = 256
MLA_KV_LORA = 128
MLA_NOPE = 64
MLA_ROPE = 32
MLA_V = 64
MLA_QK = MLA_NOPE + MLA_ROPE
MLA_WIDTH = MLA_HEADS * MLA_V
ROPE_BASE = 10000.0
MOBA_HEADS = 4
MOBA_HEAD_DIM = 64
MOBA_WIDTH = MOBA_HEADS * MOBA_HEAD_DIM
MOBA_BLOCK = 256
MOBA_TOPK = 3
Q_BLOCK = 128
REL_BUCKETS = 32
REL_MAX_DIST = 128
N_EXPERTS = 16
N_EXPERT_GROUPS = 4
EXPERTS_PER_GROUP = N_EXPERTS // N_EXPERT_GROUPS
TOPK_GROUPS = 1
TOPK_EXPERTS = 2
D_EXPERT = 512
EPS = 1e-6
IN_SIZES = (SSD_WIDTH, SSD_CONV_DIM, SSD_HEADS, MLA_Q_LORA, MLA_KV_LORA, MLA_ROPE, MOBA_WIDTH, MOBA_WIDTH, MOBA_WIDTH)
N_IN = sum(IN_SIZES)

kernel_name = "hybrid_ssd_mla_moba_moe_block"

def _rms(x):
    xf = x.astype(jnp.float32)
    return (xf * lax.rsqrt(jnp.mean(xf * xf, axis=-1, keepdims=True) + EPS)).astype(x.dtype)

def rms_norm(x, g):
    return _rms(x) * g

def rope(x):
    s, d = x.shape[1], x.shape[-1]
    half = d // 2
    inv = ROPE_BASE ** (-2.0 * jnp.arange(half, dtype=jnp.float32) / d)
    ang = jnp.arange(s, dtype=jnp.float32)[:, None] * inv[None, :]
    cos = jnp.cos(ang)[None, :, None, :]
    sin = jnp.sin(ang)[None, :, None, :]
    x1, x2 = x[..., :half], x[..., half:]
    return jnp.concatenate([x1 * cos - x2 * sin, x1 * sin + x2 * cos], axis=-1).astype(x.dtype)

def rel_bucket(n):
    max_exact = REL_BUCKETS // 2
    nf = jnp.maximum(n, max_exact).astype(jnp.float32)
    large = max_exact + (jnp.log(nf / max_exact) / math.log(REL_MAX_DIST / max_exact)
                         * (REL_BUCKETS - max_exact)).astype(jnp.int32)
    large = jnp.minimum(large, REL_BUCKETS - 1)
    return jnp.where(n < max_exact, n, large)

def causal_depthwise_conv(x, w, b):
    k, ch = w.shape
    y = lax.conv_general_dilated(x, w[:, None, :], window_strides=(1,), padding=[(k - 1, 0)],
                                 dimension_numbers=("NWC", "WIO", "NWC"), feature_group_count=ch)
    return y + b

def ssd_mixer(z, xbc, dt_raw, conv_w, conv_b, dt_bias, a_log, d_skip, norm_g):
    bsz, s, _ = z.shape
    g, r, p, n, L = SSD_GROUPS, SSD_HEADS // SSD_GROUPS, SSD_HEAD_DIM, SSD_STATE, SSD_CHUNK
    nc = s // L
    xbc = jax.nn.silu(causal_depthwise_conv(xbc, conv_w, conv_b))
    xs = xbc[..., :SSD_WIDTH].reshape(bsz, nc, L, g, r, p)
    bm = xbc[..., SSD_WIDTH:SSD_WIDTH + g * n].reshape(bsz, nc, L, g, n)
    cm = xbc[..., SSD_WIDTH + g * n:].reshape(bsz, nc, L, g, n)
    dt = jax.nn.softplus((dt_raw + dt_bias).astype(jnp.float32)).reshape(bsz, nc, L, g, r)
    a = -jnp.exp(a_log.astype(jnp.float32)).reshape(g, r)
    a_cum = jnp.cumsum(dt * a, axis=2)
    xdt = xs * dt[..., None]
    causal = jnp.tril(jnp.ones((L, L), dtype=bool))[None, None, :, :, None, None]
    seg = a_cum[:, :, :, None] - a_cum[:, :, None, :]
    decay = jnp.exp(jnp.where(causal, seg, -jnp.inf))
    cb = jnp.einsum("bclgn,bcsgn->bclsg", cm, bm)
    y_diag = jnp.einsum("bclsgr,bcsgrp->bclgrp", cb[..., None] * decay, xdt)
    to_end = jnp.exp(a_cum[:, :, -1:] - a_cum)
    states = jnp.einsum("bclgn,bclgrp->bcgrpn", bm, xdt * to_end[..., None])
    chunk_decay = jnp.exp(a_cum[:, :, -1])

    def step(h, inp):
        st, dc = inp
        return h * dc[..., None, None] + st, h

    h0 = jnp.zeros((bsz, g, r, p, n), states.dtype)
    _, h_prev = lax.scan(step, h0, (jnp.moveaxis(states, 1, 0), jnp.moveaxis(chunk_decay, 1, 0)))
    h_prev = jnp.moveaxis(h_prev, 0, 1)
    y_off = jnp.einsum("bclgn,bcgrpn->bclgrp", cm, h_prev) * jnp.exp(a_cum)[..., None]
    y = y_diag + y_off + xs * d_skip.reshape(g, r)[:, :, None]
    y = y.reshape(bsz, s, SSD_WIDTH).astype(z.dtype) * jax.nn.silu(z)
    y = _rms(y.reshape(bsz, s, g, SSD_WIDTH // g)).reshape(bsz, s, SSD_WIDTH)
    return y * norm_g

def dense_causal_attention(q, k, v, scale):
    bsz, s, h, dk = q.shape
    nq = s // Q_BLOCK
    qb = jnp.moveaxis(q.reshape(bsz, nq, Q_BLOCK, h, dk), 1, 0)
    kpos = jnp.arange(s)

    def one_block(args):
        qi, i = args
        logits = jnp.einsum("bqhd,bkhd->bhqk", qi, k).astype(jnp.float32) * scale
        qpos = i * Q_BLOCK + jnp.arange(Q_BLOCK)
        logits = jnp.where(kpos[None, :] <= qpos[:, None], logits, -jnp.inf)
        pr = jax.nn.softmax(logits, axis=-1).astype(v.dtype)
        return jnp.einsum("bhqk,bkhd->bqhd", pr, v)

    out = lax.map(one_block, (qb, jnp.arange(nq)))
    return jnp.moveaxis(out, 0, 1).reshape(bsz, s, h * v.shape[-1])

def mla_mixer(cq, ckv, krope, q_norm_g, w_uq, kv_norm_g, w_ukv, q_gain, k_gain):
    bsz, s, _ = cq.shape
    q = (rms_norm(cq, q_norm_g) @ w_uq).reshape(bsz, s, MLA_HEADS, MLA_QK)
    kv = (rms_norm(ckv, kv_norm_g) @ w_ukv).reshape(bsz, s, MLA_HEADS, MLA_NOPE + MLA_V)
    k_nope, v = kv[..., :MLA_NOPE], kv[..., MLA_NOPE:]
    q = jnp.concatenate([q[..., :MLA_NOPE], rope(q[..., MLA_NOPE:])], axis=-1)
    k_pe = jnp.broadcast_to(rope(krope[:, :, None, :]), (bsz, s, MLA_HEADS, MLA_ROPE))
    k = jnp.concatenate([k_nope, k_pe], axis=-1)
    q = rms_norm(q, q_gain)
    k = rms_norm(k, k_gain)
    return dense_causal_attention(q, k, v, MLA_QK ** -0.5)

def moba_mixer(q, k, v, q_gain, k_gain, rel_bias):
    bsz, s, _ = q.shape
    h, d, blk = MOBA_HEADS, MOBA_HEAD_DIM, MOBA_BLOCK
    q = rms_norm(q.reshape(bsz, s, h, d), q_gain)
    k = rms_norm(k.reshape(bsz, s, h, d), k_gain)
    v = v.reshape(bsz, s, h, d)
    nb = -(-s // blk)
    pad = nb * blk - s
    kblk = jnp.pad(k, ((0, 0), (0, pad), (0, 0), (0, 0))).reshape(bsz, nb, blk, h, d)
    vblk = jnp.pad(v, ((0, 0), (0, pad), (0, 0), (0, 0))).reshape(bsz, nb, blk, h, d)
    kmean = jnp.mean(kblk, axis=2)
    nq = s // Q_BLOCK
    qb = q.reshape(bsz, nq, Q_BLOCK, h, d)
    k_sel = min(MOBA_TOPK, nb)
    scale = d ** -0.5
    bias_t = rel_bias.T
    hidx3 = jnp.arange(h)[None, :, None]
    hidx4 = jnp.arange(h)[None, :, None, None]
    offs = jnp.arange(blk)

    def per_batch(args):
        qb_b, kblk_b, vblk_b, kmean_b = args
        k_by_head = jnp.moveaxis(kblk_b, 2, 0)
        v_by_head = jnp.moveaxis(vblk_b, 2, 0)

        def per_chunk(args2):
            qi, ci = args2
            qpos = ci * Q_BLOCK + jnp.arange(Q_BLOCK)
            own = (ci * Q_BLOCK) // blk
            gate = jnp.einsum("qhd,nhd->qhn", qi, kmean_b).astype(jnp.float32)
            gate = jnp.where((jnp.arange(nb) < own)[None, None, :], gate, -jnp.inf)
            top_val, top_idx = lax.top_k(gate, k_sel)
            valid = jnp.isfinite(top_val)
            gk = k_by_head[hidx3, top_idx]
            gv = v_by_head[hidx3, top_idx]
            sel = jnp.einsum("qhd,qhksd->qhks", qi, gk).astype(jnp.float32) * scale
            sel_dist = jnp.maximum(qpos[:, None, None, None] - (top_idx[..., None] * blk + offs), 0)
            sel = sel + bias_t[hidx4, rel_bucket(sel_dist)]
            sel = jnp.where(valid[..., None], sel, -jnp.inf)
            own_k = lax.dynamic_index_in_dim(kblk_b, own, axis=0, keepdims=False)
            own_v = lax.dynamic_index_in_dim(vblk_b, own, axis=0, keepdims=False)
            own_l = jnp.einsum("qhd,shd->qhs", qi, own_k).astype(jnp.float32) * scale
            dist = qpos[:, None] - (own * blk + offs)[None, :]
            own_l = own_l + jnp.moveaxis(bias_t[:, rel_bucket(jnp.maximum(dist, 0))], 0, 1)
            own_l = jnp.where((dist >= 0)[:, None, :], own_l, -jnp.inf)
            logits = jnp.concatenate([sel.reshape(Q_BLOCK, h, k_sel * blk), own_l], axis=-1)
            pr = jax.nn.softmax(logits, axis=-1).astype(v.dtype)
            p_sel = pr[..., :k_sel * blk].reshape(Q_BLOCK, h, k_sel, blk)
            p_own = pr[..., k_sel * blk:]
            return jnp.einsum("qhks,qhksd->qhd", p_sel, gv) + jnp.einsum("qhs,shd->qhd", p_own, own_v)

        return lax.map(per_chunk, (qb_b, jnp.arange(nq)))

    out = lax.map(per_batch, (qb, kblk, vblk, kmean))
    return out.reshape(bsz, s, h * d)

def moe_ffn(x, router_w, router_bias, w_gate, w_up, w_down):
    bsz, s, dm = x.shape
    t = x.reshape(-1, dm)
    scores = jax.nn.sigmoid((t @ router_w).astype(jnp.float32))
    biased = scores + router_bias.astype(jnp.float32)
    grp = biased.reshape(-1, N_EXPERT_GROUPS, EXPERTS_PER_GROUP)
    group_score = jnp.sum(lax.top_k(grp, 2)[0], axis=-1)
    _, gidx = lax.top_k(group_score, TOPK_GROUPS)
    gmask = jnp.sum(jax.nn.one_hot(gidx, N_EXPERT_GROUPS, dtype=jnp.float32), axis=-2) > 0
    emask = jnp.repeat(gmask, EXPERTS_PER_GROUP, axis=-1)
    _, eidx = lax.top_k(jnp.where(emask, biased, -jnp.inf), TOPK_EXPERTS)
    w = jnp.take_along_axis(scores, eidx, axis=-1)
    w = w / jnp.sum(w, axis=-1, keepdims=True)
    gates = jnp.sum(jax.nn.one_hot(eidx, N_EXPERTS, dtype=jnp.float32) * w[..., None], axis=-2).astype(t.dtype)
    out = jnp.zeros_like(t)
    for e in range(N_EXPERTS):
        hid = jax.nn.silu(t @ w_gate[e]) * (t @ w_up[e])
        out = out + gates[:, e:e + 1] * (hid @ w_down[e])
    return out.reshape(bsz, s, dm)

def setup_inputs(seed: int = 0) -> dict:
    key = jax.random.key(seed)
    ks = jax.random.split(key, 32)
    f32 = jnp.float32

    def nrm(k, shape, scale):
        return jax.random.normal(k, shape, f32) * scale

    def gain(k, shape):
        return 1.0 + 0.1 * jax.random.normal(k, shape, f32)

    dt = jnp.exp(jax.random.uniform(ks[9], (DEPTH, SSD_HEADS), f32, math.log(1e-3), math.log(1e-1)))
    return {
        "x": nrm(ks[0], (BATCH, SEQ, D_MODEL), 1.0),
        "c": nrm(ks[1], (BATCH, D_MODEL), 1.0),
        "ada_w": nrm(ks[2], (DEPTH, D_MODEL, 6 * D_MODEL), 0.5 * D_MODEL ** -0.5),
        "ada_b": nrm(ks[3], (DEPTH, 6 * D_MODEL), 0.02),
        "norm_mix_g": gain(ks[4], (DEPTH, D_MODEL)),
        "norm_ffn_g": gain(ks[5], (DEPTH, D_MODEL)),
        "w_in": nrm(ks[6], (DEPTH, D_MODEL, N_IN), D_MODEL ** -0.5),
        "ssd_conv_w": nrm(ks[7], (DEPTH, SSD_CONV, SSD_CONV_DIM), SSD_CONV ** -0.5),
        "ssd_conv_b": nrm(ks[8], (DEPTH, SSD_CONV_DIM), 0.02),
        "ssd_dt_bias": dt + jnp.log(-jnp.expm1(-dt)),
        "ssd_a_log": jnp.log(jax.random.uniform(ks[10], (DEPTH, SSD_HEADS), f32, 1.0, 16.0)),
        "ssd_d": gain(ks[11], (DEPTH, SSD_HEADS)),
        "ssd_norm_g": gain(ks[12], (DEPTH, SSD_WIDTH)),
        "mla_q_norm_g": gain(ks[13], (DEPTH, MLA_Q_LORA)),
        "mla_w_uq": nrm(ks[14], (DEPTH, MLA_Q_LORA, MLA_HEADS * MLA_QK), MLA_Q_LORA ** -0.5),
        "mla_kv_norm_g": gain(ks[15], (DEPTH, MLA_KV_LORA)),
        "mla_w_ukv": nrm(ks[16], (DEPTH, MLA_KV_LORA, MLA_HEADS * (MLA_NOPE + MLA_V)), MLA_KV_LORA ** -0.5),
        "mla_q_gain": gain(ks[17], (DEPTH, MLA_QK)),
        "mla_k_gain": gain(ks[18], (DEPTH, MLA_QK)),
        "mla_out_g": gain(ks[19], (DEPTH, MLA_WIDTH)),
        "moba_q_gain": gain(ks[20], (DEPTH, MOBA_HEAD_DIM)),
        "moba_k_gain": gain(ks[21], (DEPTH, MOBA_HEAD_DIM)),
        "moba_out_g": gain(ks[22], (DEPTH, MOBA_WIDTH)),
        "rel_bias": nrm(ks[23], (REL_BUCKETS, MOBA_HEADS), 0.5),
        "w_out": nrm(ks[24], (DEPTH, D_MIX, D_MODEL), D_MIX ** -0.5),
        "router_w": nrm(ks[25], (D_MODEL, N_EXPERTS), D_MODEL ** -0.5),
        "router_bias": nrm(ks[26], (N_EXPERTS,), 0.01),
        "moe_w_gate": nrm(ks[27], (DEPTH, N_EXPERTS, D_MODEL, D_EXPERT), D_MODEL ** -0.5),
        "moe_w_up": nrm(ks[28], (DEPTH, N_EXPERTS, D_MODEL, D_EXPERT), D_MODEL ** -0.5),
        "moe_w_down": nrm(ks[29], (DEPTH, N_EXPERTS, D_EXPERT, D_MODEL), D_EXPERT ** -0.5),
    }

def reference(x, c, ada_w, ada_b, norm_mix_g, norm_ffn_g, w_in, ssd_conv_w, ssd_conv_b, ssd_dt_bias,
              ssd_a_log, ssd_d, ssd_norm_g, mla_q_norm_g, mla_w_uq, mla_kv_norm_g, mla_w_ukv, mla_q_gain,
              mla_k_gain, mla_out_g, moba_q_gain, moba_k_gain, moba_out_g, rel_bias, w_out, router_w,
              router_bias, moe_w_gate, moe_w_up, moe_w_down):
    split_at = np.cumsum(IN_SIZES)[:-1].tolist()
    c_act = jax.nn.silu(c)
    for l in range(DEPTH):
        mod = (c_act @ ada_w[l] + ada_b[l])[:, None, :]
        sh_m, sc_m, g_m, sh_f, sc_f, g_f = jnp.split(mod, 6, axis=-1)
        hm = rms_norm(x, norm_mix_g[l]) * (1.0 + sc_m) + sh_m
        proj = hm @ w_in[l]
        z, xbc, dt_raw, cq, ckv, krope, mq, mk, mv = jnp.split(proj, split_at, axis=-1)
        y_ssd = ssd_mixer(z, xbc, dt_raw, ssd_conv_w[l], ssd_conv_b[l], ssd_dt_bias[l], ssd_a_log[l],
                          ssd_d[l], ssd_norm_g[l])
        y_mla = rms_norm(mla_mixer(cq, ckv, krope, mla_q_norm_g[l], mla_w_uq[l], mla_kv_norm_g[l],
                                   mla_w_ukv[l], mla_q_gain[l], mla_k_gain[l]), mla_out_g[l])
        y_moba = rms_norm(moba_mixer(mq, mk, mv, moba_q_gain[l], moba_k_gain[l], rel_bias), moba_out_g[l])
        y = jnp.concatenate([y_ssd, y_mla, y_moba], axis=-1) @ w_out[l]
        x = x + g_m * y
        hf = rms_norm(x, norm_ffn_g[l]) * (1.0 + sc_f) + sh_f
        x = x + g_f * moe_ffn(hf, router_w, router_bias, moe_w_gate[l], moe_w_up[l], moe_w_down[l])
    return x


_drawn_inputs = setup_inputs


def setup_inputs(seed=0):
    import zlib

    import numpy as np

    out = dict(_drawn_inputs(seed))
    spreads = {}
    factors = {'ssd_conv_b': 3.75, 'mla_q_gain': 2.685, 'mla_k_gain': 3.075, 'moba_q_gain': 3.334}
    for name, (base, spread) in spreads.items():
        noise = np.random.default_rng([zlib.crc32(name.encode()), seed]).standard_normal(out[name].shape)
        drawn = base * np.exp(spread * noise) if base else spread * noise
        out[name] = __import__('jax').numpy.asarray(drawn.astype(out[name].dtype))
    for name, factor in factors.items():
        out[name] = (out[name] * factor).astype(out[name].dtype)
    return out
```

```python
from contextlib import ExitStack

import numpy as np

import concourse.bass as bass
from concourse import mybir

F32 = mybir.dt.float32
F32R = mybir.dt.float32r
I32 = mybir.dt.int32
ACT = mybir.ActivationFunctionType
ALU = mybir.AluOpType
AX = mybir.AxisListType

P = 128
S, D, DEPTH = 512, 1024, 2
T = S // P
KD = D // P
NH, HP, NST = 8, 64, 128
NIN = 2728
MH, DQ, DN, DR, DV = 4, 96, 64, 32, 64
NE, DE = 16, 512
NOV = 7
NT = 24
EPS = 1e-6
NEG = -1e30
MAXD = S - 1

Z0, DT0, CQ0, CKV0, KR0, MQ0, MK0, MV0, NPROJ = 0, 512, 520, 776, 904, 936, 1192, 1448, 1704

C_ID, C_TRI, C_NEG, C_STR, C_ONE, C_MASK = 0, 128, 256, 384, 512, 640
C_COS, C_SIN = 1152, 1216
C_EPS, C_REV4, C_REV16, C_IOTA16, C_IOTA7, C_UP = 1280, 1281, 1285, 1301, 1317, 1324
C_IOTA = C_UP + 33
C_TOK = C_IOTA + P
C_N = C_TOK + T


def shape_constants():
    c = np.zeros((P, C_N), np.float32)
    i = np.arange(P)
    c[:, C_ID:C_ID + P] = np.eye(P)
    c[:, C_TRI:C_TRI + P] = i[:, None] <= i[None, :]
    c[:, C_NEG:C_NEG + P] = np.where(i[:, None] <= i[None, :], 0.0, NEG)
    c[:, C_STR:C_STR + P] = i[:, None] < i[None, :]
    c[:, C_ONE:C_ONE + P] = 1.0
    m = np.arange(S)
    c[:, C_MASK:C_MASK + S] = np.where(m[None, :] <= i[:, None] + S - P, 0.0, NEG)
    half = DR // 2
    inv = np.float32(10000.0) ** (np.float32(-2.0) * np.arange(half, dtype=np.float32) / np.float32(DR))
    ang = np.arange(S, dtype=np.float32)[:, None] * inv[None, :].astype(np.float32)
    c[:, C_COS:C_COS + 64] = np.cos(ang).reshape(T, P, half).transpose(1, 0, 2).reshape(P, 64)
    c[:, C_SIN:C_SIN + 64] = np.sin(ang).reshape(T, P, half).transpose(1, 0, 2).reshape(P, 64)
    c[:, C_EPS] = EPS
    c[:, C_REV4:C_REV4 + 4] = 4 - np.arange(4)
    c[:, C_REV16:C_REV16 + 16] = 16 - np.arange(16)
    c[:, C_IOTA16:C_IOTA16 + 16] = np.arange(16)
    c[:, C_IOTA7:C_IOTA7 + 7] = np.arange(7)
    c[:, C_IOTA:C_IOTA + P] = np.arange(P)
    c[:, C_TOK:C_TOK + T] = P * np.arange(T)[None, :] + i[:, None]
    e = np.arange(NE)
    c[:NE, C_UP:C_UP + 16] = e[:, None] < e[None, :]
    c[:NE, C_UP + 16] = 1.0
    c[:NE, C_UP + 17:C_UP + 33] = e[:, None] <= e[None, :]
    dist = MAXD - np.arange(640)
    n = np.maximum(dist, 0)
    large = 16 + (np.log(np.maximum(n, 16).astype(np.float32) / np.float32(16))
                  / np.float32(np.log(8.0)) * np.float32(16)).astype(np.int32)
    bucket = np.where(n < 16, n, np.minimum(large, 31))
    oh = np.zeros((33, 640 + 4), np.float32)
    oh[bucket[dist >= 0], np.arange(640)[dist >= 0]] = 1.0
    oh[32, :640][dist < 0] = 1.0
    oh[32, 640:] = NEG
    return c, oh


class Counted:

    def __init__(self, eng, sem):
        self.eng, self.sem, self.n = eng, sem, 0

    def __call__(self, ins):
        ins.then_inc(self.sem, 1)
        self.n += 1
        self.eng.wait_ge(self.sem, self.n)


def trunk(nc, A, out, cpack, bucket_oh, relv, hf_rows, y_rows):
    ctx = ExitStack()

    address = {}

    def sb(name, shape, dt=F32):
        address[name] = -(-nc.sbuf_base // 32) * 32
        return ctx.enter_context(nc.sbuf_tensor(name, shape, dt))

    sems = []

    def sem(name):
        sems.append(ctx.enter_context(nc.semaphore(name)))
        return sems[-1]

    x = sb("x", [P, T, D])
    mod = sb("mod", [P, 6 * D])
    gain = sb("gain", [P, D])
    actT = sb("actT", [P, KD, S])
    cst = sb("cst", [P, C_N])
    biasm = sb("biasm", [P, MH, S])
    rw = sb("rw", [P, KD, NE])
    rbias = sb("rbias", [P, NE])
    csil = sb("csil", [P, KD])
    prow = sb("prow", [64, P])
    pcol = sb("pcol", [P, 64])
    hpar = sb("hpar", [P, 3, NH])
    sml = sb("sml", [P, 1024])
    slot_idx = sb("slot_idx", [P, NT], I32)
    pos_i = sb("pos_i", [P, 2, T], I32)
    ctl = sb("ctl", [1, 1 + NOV], I32)
    turn_mark = sb("turn_mark", [1, 1], I32)
    ring = sb("ring", [P, 3, 4096])
    work = sb("work", [P, 20480])

    mod_r, actT_r, ring_r, work_r = (
        nc.alloc_sbuf_tensor_at(name + "_rounded", shape, F32R, offset=address[name])
        for name, shape in (("mod", [P, 6 * D]), ("actT", [P, KD, S]), ("ring", [P, 3, 4096]), ("work", [P, 20480])))

    def view(off, *dims, of=work):
        n = int(np.prod(dims))
        v = of[:, off:off + n]
        if len(dims) == 2:
            return v.rearrange("p (a b) -> p a b", a=dims[0])
        if len(dims) == 3:
            return v.rearrange("p (a b c) -> p a b c", a=dims[0], b=dims[1])
        return v

    proj = view(0, T, NPROJ)
    XB = 516
    xbcT = view(6816, 8, XB)
    kv = view(6816, T, 512)
    s0 = 10944
    xs = view(s0, 2, 512)
    xdt = view(s0 + 1024, 2, 512)
    xde = view(s0 + 2048, 2, 512)
    bmcb = view(s0 + 3072, 2, 512)
    seg = view(s0 + 4096, 2, 512)
    mt = view(s0 + 5120, 2, 512)
    yt = view(s0 + 6144, 2, 512)
    hst = view(s0 + 7168, 512)
    xd = view(18432 + 1024, 512)
    qn = view(s0, 2, T * DQ)
    kn = view(s0 + 768, 2, T * DQ)
    qT = view(s0 + 1536, 2, 512)
    kT = view(s0 + 2560, 2, 512)
    ssb = view(s0 + 3584, 2, 512)
    psb = view(s0 + 4608, 2, 512)
    pT = view(s0 + 5632, 2, 512)
    sq = view(s0 + 1536, 1536)
    rtmp = view(s0 + 3584, 4, 320)
    hrow = view(18432, 2, D)
    hfrow = view(12288, T, D)

    def h_row(base, t):
        return hfrow[:, t, :] if base else hrow[:, t % 2, :]

    ws = view(16384, 2, 512)
    cqT = actT[:, 0:3, :]
    qrow = actT[:, 3:6, :].rearrange("p a b -> p (a b)").rearrange("p (t n) -> p t n", t=T)
    slots = [ring[:, n, :] for n in range(3)] + [view(4096 * n, 4096) for n in range(3)]
    xg = view(12288, 2, D)
    xeT = view(14336, KD, P)
    sg = view(15360, 512)
    hid = view(15872, 512)
    ysb = view(16384, 2, D)
    hT = view(18432, 4, P)
    xeT_r = view(14336, KD, P, of=work_r)
    xeL = view(18944, KD, P, of=work_r)
    slots_r = [ring_r[:, n, :] for n in range(3)] + [view(4096 * n, 4096, of=work_r) for n in range(3)]
    hi_parts = [(0, 0, 4, mod_r[:, 0:2048]), (0, 4, 8, mod_r[:, 2048:4096]), (1, 0, 2, mod_r[:, 4096:5120]),
                (1, 2, 8, actT_r[:, 2:8, :].rearrange("p a b -> p (a b)"))]

    def hi_chunk(j, k):
        _, a0, _, buf = next(h for h in hi_parts if h[0] == j and h[1] <= k < h[2])
        return buf[:, 512 * (k - a0):512 * (k - a0) + 512]


    def sv(off, n):
        return sml[:, off:off + n]

    ss_x, rs_x = sv(0, 4), sv(4, 4)
    u, au, ex, y1, r1, dt, dta = (sv(8 + 32 * k, 32) for k in range(7))
    eac, tend, cd, lny = (sv(264 + 32 * k, 32) for k in range(4))
    cums = sv(740, 64)
    acs, tot = cums[:, 0:32], cums[:, 32:64]
    ealog = sv(392, 8)
    ss_c, rs_c = sv(400, 8), sv(408, 8)
    ss_h, rs_h = sv(416, 64), sv(480, 64)
    ss_y, rs_y = sv(544, 16), sv(560, 16)
    mx, lsum, linv = sv(576, 8), sv(584, 8), sv(592, 4)
    ss_kr = sv(596, 4)
    route = actT[:, 0:2, :].rearrange("p a b -> p (a b)").rearrange("p (k n) -> p k n", k=16)
    sc, bi, mb, oh1, oh2, both, eqw, jt, rowf, tmpr, tmps = (route[:, k, :] for k in range(11))
    oh12 = route[:, 3:5, :]
    oh_v = actT[:, 5, 0:128].rearrange("p (a n) -> p a n", a=2)
    tilef = actT[:, 5, 128:192]
    row_oh = actT[:, 2:4, :].rearrange("p a b -> p (a b)").rearrange("p (m n) -> p m n", m=2 * T)
    tile_tok = actT[:, 4, 0:2 * T * NT].rearrange("p (m n) -> p m n", m=2 * T)
    mm2 = route[:, 11, :]
    gs, gsel, gw = route[:, 12, 0:16], route[:, 12, 16:32], route[:, 12, 32:48]
    red = route[:, 13, :]
    w12 = route[:, 14, 0:8].rearrange("p (a t) -> p a t", a=2)
    wsum, pf = route[:, 14, 8:12], route[:, 14, 16:24].rearrange("p (a t) -> p a t", a=2)
    ov = route[:, 14, 24:25]
    ovb, c1 = route[:, 15, 0:33], route[:, 15, 40:56]
    ctf = route[:, 14, 32:40]
    rf, tf = (route[:, 14, n:n + 8].rearrange("p (a t) -> p a t", a=2) for n in (40, 48))
    cmp7 = sv(624, 112)

    ps = [ctx.enter_context(nc.psum_tensor(f"ps{n}", [P, 512], F32)) for n in range(8)]

    ident = cst[:, C_ID:C_ID + P]
    tri = cst[:, C_TRI:C_TRI + P]
    negt = cst[:, C_NEG:C_NEG + P]
    stri = cst[:, C_STR:C_STR + P]
    ones = cst[:, C_ONE:C_ONE + P]
    epsc = cst[:, C_EPS:C_EPS + 1]

    par = sem("small_params_loaded")
    gain_ld = sem("gain_loaded")
    modb_ld = sem("mod_bias_loaded")
    slot_ld = [sem(f"slot{n}_loaded") for n in range(6)]
    vch = sem("vector_step")
    ach = sem("scalar_step")
    gch = sem("gpsimd_step")
    acc_ps = sem("acc_in_psum")
    ada_ev = sem("ada_block_out")
    win_ev = sem("w_in_block_out")
    wo_ev = sem("w_out_block_out")
    pcol_ps = sem("params_transposed")
    pcol_sb = sem("params_in_columns")
    xss = sem("x_squares_summed")
    g_used = sem("gain_used")
    hrow_dn = sem("h_row_done")
    h_ps = sem("h_transposed")
    h_ev = sem("h_columns_out")
    pads = sem("conv_pads_zeroed")
    conv_dn = sem("conv_sum_done")
    silu_dn = sem("conv_silu_done")
    sp_u = sem("dt_abs_done")
    sp_e = sem("dt_exp_done")
    sp_y = sem("dt_one_plus_exp_done")
    sp_l = sem("dt_log_done")
    dta_dn = sem("dta_done")
    cum_ps = sem("cumsum_in_psum")
    cum_sb = sem("cumsum_copied")
    tend_d = sem("to_end_difference_done")
    cume = sem("cumsum_exponentials_done")
    c_ss = sem("latent_rstd_done")
    c_nm = sem("latent_normed")
    c_ps = sem("latent_transposed")
    c_ev = sem("latent_columns_out")
    xs_ps = sem("xs_rows_in_psum")
    bm_ps = sem("b_rows_and_cb_in_psum")
    dec_ps = sem("decay_log_in_psum")
    xs_cp = sem("xs_rows_copied")
    bm_cp = sem("b_rows_and_cb_copied")
    xde_dn = sem("xdt_done")
    seg_dn = sem("decay_difference_done")
    seg_ex = sem("decay_exponential_done")
    m_dn = sem("ssd_scores_done")
    yd_ps = sem("y_diag_in_psum")
    yo_ps = sem("y_off_in_psum")
    st_ps = sem("state_in_psum")
    h_dn = sem("state_updated")
    xd_dn = sem("skip_product_done")
    y_dn = sem("ssd_chunk_done")
    ysq = sem("ssd_squares_summed")
    yrs = sem("ssd_rstd_done")
    qkv_ps = sem("mla_qkv_in_psum")
    qkv_ev = sem("mla_qkv_copied")
    kr_dn = sem("rope_done")
    hss = sem("head_squares_summed")
    hrs = sem("head_rstd_done")
    stg = sem("head_staged")
    qk_ps = sem("qk_transposed")
    q_sb = sem("q_columns_out")
    k_sb = sem("k_columns_out")
    s_ps = sem("scores_in_psum")
    s_sb = sem("scores_biased_and_max")
    p_dn = sem("probs_done")
    pt_ps = sem("probs_transposed")
    pt_ev = sem("probs_columns_out")
    pv_ps = sem("pv_in_psum")
    o_dn = sem("head_output_done")
    yss = sem("mixer_rstd_done")
    yn = sem("mixer_normed")
    yc_ps = sem("mixer_transposed")
    yc_ev = sem("mixer_columns_out")
    hf_wr = sem("ffn_rows_stored")
    rt_ps = sem("router_in_psum")
    rt_ex = sem("router_exp_done")
    both_dn = sem("choice_done")
    rk_ps = sem("ranks_in_psum")
    ov_dn = sem("further_tiles_counted")
    ovb_ps = sem("further_tiles_in_psum")
    pos_dn = sem("positions_done")
    sel_dn = sem("slot_selectors_done")
    tab_ps = sem("slot_table_in_psum")
    tab_sb = sem("slot_table_out")
    gat = [sem(f"tokens_gathered{n}") for n in range(2)]
    xt_ps = sem("expert_tokens_transposed")
    xt_ev = sem("expert_tokens_columns_out")
    xl_dn = sem("expert_tokens_low_done")
    w_hi = sem("weights_high_done")
    w_lo = sem("weights_low_done")
    gu_ps = sem("gate_up_in_psum")
    sil = sem("gate_silu_done")
    hid_dn = sem("hidden_done")
    ht_ps = sem("hidden_transposed")
    ht_ev = sem("hidden_columns_out")
    y_ps = sem("expert_out_in_psum")
    y_ev = sem("expert_out_scaled")
    yw = [sem(f"expert_out_stored{n}") for n in range(2)]
    turn = sem("further_tile_turn")
    ov_w = sem("further_weights_loaded")
    ov_g = sem("further_tokens_gathered")
    ov_xp = sem("further_tokens_transposed")
    ov_xe = sem("further_tokens_out")
    ov_gu = sem("further_gate_up_in_psum")
    ov_si = sem("further_silu_done")
    ov_hd = sem("further_hidden_done")
    ov_hp = sem("further_hidden_transposed")
    ov_he = sem("further_hidden_out")
    ov_yp = sem("further_out_in_psum")
    ov_ye = sem("further_out_scaled")
    ov_yw = sem("further_out_stored")
    cg = [sem(f"choices_gathered{n}") for n in range(2)]
    cdn = sem("token_tile_combined")
    first, last = sems[0].num, sems[-1].num
    assert last - first == len(sems) - 1

    with nc.Block() as block:
        @block.sync
        def _(sp):
            sp.dma_start(cst[:], cpack).then_inc(par, 16)
            sp.dma_start(work[0:33, 0:644], bucket_oh).then_inc(par, 16)
            sp.dma_start(sml[0:32, 0:4], A["rel_bias"]).then_inc(gain_ld, 16)
            sp.dma_start(prow[0:KD, :], A["c"].rearrange("a (k p) -> (a k) p", p=P)).then_inc(modb_ld, 16)
            sp.dma_start(x[:], A["x"].rearrange("a (t p) d -> p (a t) d", p=P)).then_inc(slot_ld[0], 16)
            sp.dma_start(rw[:], A["router_w"].rearrange("(k p) e -> p k e", p=P)).then_inc(slot_ld[0], 16)
            sp.dma_start(rbias[:], A["router_bias"].rearrange("(a e) -> a e", a=1).broadcast_to([P, NE])
                         ).then_inc(slot_ld[0], 16)
            sp.wait_ge(gch, 1)
            sp.dma_start(y_rows.rearrange("(p n) d -> p n d", n=NT)[:, NE:NT, :],
                         work[:, 2048:2048 + D].unsqueeze(1).to_broadcast([P, NT - NE, D])).then_inc(slot_ld[2], 16)
            sp.wait_ge(ach, 2)
            sp.dma_start(relv, work[0:MH, 1024:1664].unsqueeze(1).to_broadcast([MH, P, 640])).then_inc(slot_ld[1], 16)
            sp.wait_ge(slot_ld[1], 16)
            src = bass.AP(tensor=relv.tensor, offset=relv.offset + P - 1, ap=[[639, P], [P * 640, MH], [1, S]])
            sp.dma_start(biasm[:], src).then_inc(slot_ld[1], 16)
            sp.wait_ge(slot_ld[1], 32)
            sp.wait_ge(slot_ld[0], 48)
            sp.wait_ge(slot_ld[2], 16)

        @block.tensor
        def _(pe):
            pe.wait_ge(par, 32)
            pe.wait_ge(gain_ld, 16)
            pe.wait_ge(vch, 1)
            pe.matmul(ps[0][0:MH, :], sml[0:33, 0:4], work[0:33, 0:512], start=True, stop=True)
            pe.matmul(ps[1][0:MH, 0:128], sml[0:33, 0:4], work[0:33, 512:640], start=True, stop=True
                      ).then_inc(acc_ps, 1)
            pe.wait_ge(modb_ld, 16)
            pe.transpose(ps[2][:, 0:KD], prow[0:KD, :], cst[0:KD, C_ID:C_ID + KD]).then_inc(acc_ps, 1)

        @block.vector
        def _(v):
            v.wait_ge(par, 32)
            v.tensor_copy(sml[32:33, 0:4], work[32:33, 640:644]).then_inc(vch, 1)

        @block.scalar
        def _(a):
            a.wait_ge(acc_ps, 1)
            a.activation(work[0:MH, 1024:1536], ps[0][0:MH, :], ACT.Copy).then_inc(ach, 1)
            a.activation(work[0:MH, 1536:1664], ps[1][0:MH, 0:128], ACT.Copy).then_inc(ach, 1)
            a.wait_ge(acc_ps, 2)
            a.activation(csil[:], ps[2][:, 0:KD], ACT.Silu).then_inc(ach, 1)

        @block.gpsimd
        def _(g):
            g.memset(work[:, 2048:2048 + D], 0.0).then_inc(gch, 1)
    nc.all_engine_barrier(sems_to_clear=range(first, last + 1))

    mixer_loads = [("ada", b) for b in range(4)] + [("in", b) for b in (1, 2, 3, 0, 4, 5)] \
        + [("ada", 4), ("ada", 5), ("mla", 0)] + [("ada", b) for b in range(6, 11)] \
        + [("out", 0), ("out", 1), ("ada", 11)]
    NML = len(mixer_loads)
    assert NML % 3 == 0
    load_no = {what: n for n, what in enumerate(mixer_loads)}
    in_width = [min(512, NIN - 512 * b) for b in range(6)]
    groups = [("ada", b, 0) for b in range(4)] + [("in", b, t) for b in (1, 2, 3, 0, 4, 5) for t in range(T)] \
        + [("ada", b, 0) for b in range(4, 11)] + [("out", b, t) for t in range(T) for b in range(2)] \
        + [("ada", 11, 0)]
    group_no = {g: n for n, g in enumerate(groups)}

    def slot_read(n):
        what, b = mixer_loads[n]
        if what == "mla":
            return qkv_ps, 2 * T
        return acc_ps, 1 + max(m for m, g in enumerate(groups) if g[:2] == (what, b))

    def out_before(n, kind):
        return sum(1 for g in groups[:n] if g[0] == kind)

    DQK = [DQ] * MH + [HP] * MH
    o_col = [CQ0 + DV * h for h in range(MH)] + [MQ0 + HP * h for h in range(MH)]
    y_col = [0, 128, 256, 384, CQ0, CQ0 + 128, MQ0, MQ0 + 128]

    base_ld = [16 * (NML // 3 + 1) + (16 if load_no[("mla", 0)] % 3 == j else 0) for j in range(3)]

    def expert_loaded(e, odd, j):
        return slot_ld[3 * odd + j], 8 * (e + 1) if odd else 8 * e + base_ld[j]

    with nc.Fori(0, DEPTH) as L:
        def at_layer(ap, names="a n"):
            return ap[bass.ds(L, 1)]

        with nc.Block() as block:
            @block.sync
            def _(sp):
                def load(what, b, n):
                    slot = slots[n % 3]
                    if n >= 3:
                        sp.wait_ge(*slot_read(n - 3))
                    if what == "ada":
                        src = A["ada_w"][bass.ds(L, 1), :, 512 * b:512 * b + 512].rearrange("l (k p) n -> p (l k) n", p=P)
                        dst = slot.rearrange("p (k n) -> p k n", k=KD)
                    elif what == "in":
                        w = in_width[b]
                        src = A["w_in"][bass.ds(L, 1), :, 512 * b:512 * b + w].rearrange("l (k p) n -> p (l k) n", p=P)
                        dst = slot[:, 0:KD * w].rearrange("p (k n) -> p k n", k=KD)
                    elif what == "out":
                        src = A["w_out"][bass.ds(L, 1), :, 512 * b:512 * b + 512].rearrange("l (k p) n -> p (l k) n", p=P)
                        dst = slot.rearrange("p (k n) -> p k n", k=KD)
                    else:
                        src = A["mla_w_uq"][bass.ds(L, 1)].rearrange("l (k p) n -> p (l k) n", p=P)
                        sp.dma_start(slot[:, 0:768].rearrange("p (k n) -> p k n", k=2), src).then_inc(slot_ld[n % 3], 16)
                        src = A["mla_w_ukv"][bass.ds(L, 1)].rearrange("l p n -> p (l n)")
                        dst = slot[:, 768:1280]
                    sp.dma_start(dst, src).then_inc(slot_ld[n % 3], 16)

                sp.wait_ge(pads, 1)
                rows = [(A["ssd_conv_w"][bass.ds(L, 1)].rearrange("l k (f p) -> (l k f) p", p=P), 0, 32, P),
                        (A["ssd_conv_b"][bass.ds(L, 1)].rearrange("l (f p) -> (l f) p", p=P), 32, 8, P),
                        (A["mla_q_norm_g"][bass.ds(L, 1)].rearrange("l (f p) -> (l f) p", p=P), 40, 2, P),
                        (A["mla_kv_norm_g"][bass.ds(L, 1)].rearrange("l (f p) -> (l f) p", p=P), 42, 1, P),
                        (A["ssd_norm_g"][bass.ds(L, 1)].rearrange("l (f p) -> (l f) p", p=P), 43, 4, P),
                        (A["mla_out_g"][bass.ds(L, 1)].rearrange("l (f p) -> (l f) p", p=P), 47, 2, P),
                        (A["moba_out_g"][bass.ds(L, 1)].rearrange("l (f p) -> (l f) p", p=P), 49, 2, P),
                        (A["mla_q_gain"][bass.ds(L, 1)], 51, 1, DQ), (A["mla_k_gain"][bass.ds(L, 1)], 52, 1, DQ),
                        (A["moba_q_gain"][bass.ds(L, 1)], 53, 1, HP), (A["moba_k_gain"][bass.ds(L, 1)], 54, 1, HP)]
                load("ada", 0, 0)
                sp.dma_start(mod[:], A["ada_b"][bass.ds(L, 1)].broadcast_to([P, 6 * D])).then_inc(modb_ld, 16)
                load("ada", 1, 1)
                sp.dma_start(gain[:], A["norm_mix_g"][bass.ds(L, 1)].broadcast_to([P, D])).then_inc(gain_ld, 16)
                load("ada", 2, 2)
                for src, r0, nr, w in rows:
                    sp.dma_start(prow[r0:r0 + nr, 0:w], src).then_inc(par, 16)
                for n, name in enumerate(("ssd_dt_bias", "ssd_a_log", "ssd_d")):
                    sp.dma_start(hpar[:, n, :], A[name][bass.ds(L, 1)].broadcast_to([P, NH])).then_inc(par, 16)
                for n, (what, b) in enumerate(mixer_loads):
                    if n >= 3:
                        load(what, b, n)
                    if n == 12:
                        sp.wait_ge(g_used, 1)
                        sp.dma_start(gain[:], A["norm_ffn_g"][bass.ds(L, 1)].broadcast_to([P, D])).then_inc(gain_ld, 16)

                w_gate = A["moe_w_gate"].rearrange("l e (k p) n -> (l e) p k n", p=P)
                w_up = A["moe_w_up"].rearrange("l e (k p) n -> (l e) p k n", p=P)
                w_down = A["moe_w_down"].rearrange("l e (k p) n -> (l e) p k n", p=P)

                def expert(e, odd, wait):
                    for j, (w, k) in enumerate(((w_gate, KD), (w_up, KD), (w_down, 4))):
                        if wait:
                            if j < 2:
                                sp.wait_ge(gu_ps, 2 * (e - 1))
                            else:
                                sp.wait_ge(y_ps, 2 * (e - 1))
                        elif not odd:
                            sp.wait_ge(*slot_read(NML - 3 + j))
                        n = 3 * odd + j
                        sp.dma_start(slots[n].rearrange("p (k n) -> p k n", k=k),
                                     w[bass.ds(L * NE + e, 1)].rearrange("o p k n -> p (o k) n")
                                     ).then_inc(slot_ld[n], 16)

                expert(0, 0, False)
                sp.wait_ge(wo_ev, 8)
                expert(1, 1, False)
                with sp.Fori(0, NE // 2 - 1) as i:
                    expert(2 * i + 2, 0, True)
                    expert(2 * i + 3, 1, True)
                sp.wait_ge(pos_dn, 2)
                nov = sp.value_load(ctl[0:1, 0:1], min_val=0, max_val=NOV)
                with sp.Fori(0, NOV) as i:
                    with sp.If(nov > i):
                        sp.wait_ge(turn, i + 1)
                        eid = sp.value_load(ctl[0:1, bass.ds(i + 1, 1)], min_val=0, max_val=NE - 1)
                        for j, (w, k) in enumerate(((w_gate, KD), (w_up, KD), (w_down, 4))):
                            sp.dma_start(slots[j].rearrange("p (k n) -> p k n", k=k),
                                         w[bass.ds(L * NE + eid, 1)].rearrange("o p k n -> p (o k) n")
                                         ).then_inc(ov_w, 16)

            @block.tensor
            def _(pe):
                def slot_of(what, b):
                    n = load_no[(what, b)]
                    extra = 16 if n % 3 == load_no[("mla", 0)] % 3 and n >= load_no[("mla", 0)] else 0
                    pe.wait_ge(slot_ld[n % 3], 16 * (n // 3 + 1) + extra)
                    return slots[n % 3]

                def bank_free(n):
                    if n >= 2:
                        kind = groups[n - 2][0]
                        pe.wait_ge({"ada": ada_ev, "in": win_ev, "out": wo_ev}[kind], out_before(n - 1, kind))

                def ada(b):
                    n = group_no[("ada", b, 0)]
                    w = slot_of("ada", b).rearrange("p (k n) -> p k n", k=KD)
                    bank_free(n)
                    for k in range(KD):
                        mm = pe.matmul(ps[n % 2][:, :], csil[:, k:k + 1].to_broadcast([P, P]), w[:, k, :],
                                       start=k == 0, stop=k == KD - 1)
                        if k == KD - 1:
                            mm.then_inc(acc_ps, 1)

                for b in range(4):
                    ada(b)
                pe.wait_ge(par, 14 * 16)
                pe.transpose(ps[2][:, 0:64], prow[:], cst[0:64, C_ID:C_ID + 64]).then_inc(pcol_ps, 1)
                pe.wait_ge(pcol_sb, 1)

                def to_columns(base, behind=None):
                    for t in range(T):
                        pe.wait_ge(hrow_dn, base + t + 1)
                        if base + t > 0:
                            pe.wait_ge(h_ev, 2 * (base + t))
                        for j in range(2):
                            for k in range(4):
                                tr = pe.transpose(ps[2 + j][:, P * k:P * k + P],
                                                  h_row(base, t)[:, P * (4 * j + k):P * (4 * j + k) + P], ident)
                            tr.then_inc(h_ps, 1)
                        if behind is not None and t > 0:
                            behind(t - 1)

                to_columns(0)
                pe.wait_ge(h_ev, 2 * T)
                for b in (1, 2, 3, 0, 4, 5):
                    wd = in_width[b]
                    w = slot_of("in", b)[:, 0:KD * wd].rearrange("p (k n) -> p k n", k=KD)
                    for t in range(T):
                        n = group_no[("in", b, t)]
                        bank_free(n)
                        for k in range(KD):
                            if b in (1, 2):
                                mm = pe.matmul(ps[n % 2][:, :], w[:, k, P * t:P * t + P], actT[:, k, :],
                                               start=k == 0, stop=k == KD - 1)
                            else:
                                mm = pe.matmul(ps[n % 2][:, 0:wd], actT[:, k, P * t:P * t + P], w[:, k, :],
                                               start=k == 0, stop=k == KD - 1)
                        mm.then_inc(acc_ps, 1)
                ada(4)
                ada(5)

                pe.wait_ge(dta_dn, 1)
                pe.matmul(ps[2][:, 0:32], tri, dta, start=True, stop=True)
                pe.matmul(ps[2][:, 32:64], ones, dta, start=True, stop=True).then_inc(cum_ps, 1)
                pe.wait_ge(c_nm, 1)
                for j in range(3):
                    for t in range(T):
                        tr = pe.transpose(ps[3 + j][:, P * t:P * t + P],
                                          proj[:, t, CQ0 + P * j:CQ0 + P * j + P], ident)
                    tr.then_inc(c_ps, 1)
                pe.wait_ge(cume, 3)
                pe.wait_ge(c_ev, 3)
                pe.wait_ge(silu_dn, 8)

                for c in range(T):
                    cs = slice(3 + P * c, 3 + P * c + P)
                    if c > 0:
                        pe.wait_ge(xs_cp, c)
                    for f in range(4):
                        tr = pe.transpose(ps[2][:, P * f:P * f + P], xbcT[:, f, cs], ident)
                    tr.then_inc(xs_ps, 1)
                    if c > 0:
                        pe.wait_ge(bm_cp, c)
                    for g in range(2):
                        pe.transpose(ps[3][:, P * g:P * g + P], xbcT[:, 4 + g, cs], ident)
                    for g in range(2):
                        mm = pe.matmul(ps[3][:, 256 + P * g:256 + P * g + P], xbcT[:, 4 + g, cs], xbcT[:, 6 + g, cs],
                                       start=True, stop=True)
                    mm.then_inc(bm_ps, 1)
                    for g in range(2):
                        if c > 0:
                            pe.wait_ge(seg_dn, 2 * (c - 1) + g + 1)
                        for h in range(4):
                            col = 8 * c + 4 * g + h
                            pe.matmul(ps[4 + g][:, P * h:P * h + P], ident, negt, start=True, stop=False)
                            mm = pe.matmul(ps[4 + g][:, P * h:P * h + P], dta[:, col:col + 1].to_broadcast([P, P]), tri,
                                           start=False, stop=True)
                        mm.then_inc(dec_ps, 1)
                    if c == 0:
                        pe.wait_ge(ada_ev, 6)
                    if c < T - 1:
                        pe.wait_ge(bm_cp, c + 1)
                        pe.wait_ge(xde_dn, c + 1)
                        if c > 0:
                            pe.wait_ge(h_dn, c)
                        for g in range(2):
                            mm = pe.matmul(ps[0][:, 256 * g:256 * g + 256], bmcb[:, c % 2, P * g:P * g + P],
                                           xde[:, c % 2, 256 * g:256 * g + 256], start=True, stop=True)
                        mm.then_inc(st_ps, 1)
                    if c > 0:
                        pe.wait_ge(h_dn, c)
                        pe.wait_ge(y_dn, c)
                        for g in range(2):
                            mm = pe.matmul(ps[7][:, 256 * g:256 * g + 256], xbcT[:, 6 + g, cs],
                                           hst[:, 256 * g:256 * g + 256], start=True, stop=True)
                        mm.then_inc(yo_ps, 1)
                    pe.wait_ge(m_dn, 2 * c + 2)
                    pe.wait_ge(xde_dn, c + 1)
                    for g in range(2):
                        for h in range(4):
                            hh = 4 * g + h
                            mm = pe.matmul(ps[6][:, HP * hh:HP * hh + HP], mt[:, g, P * h:P * h + P],
                                           xdt[:, c % 2, HP * hh:HP * hh + HP], start=True, stop=True)
                    mm.then_inc(yd_ps, 1)

                w = slot_of("mla", 0)
                wq = w[:, 0:768].rearrange("p (k n) -> p k n", k=2)
                wkv = w[:, 768:1280]
                pe.wait_ge(y_dn, 4)
                pe.wait_ge(seg_dn, 8)
                pe.wait_ge(xs_cp, 4)
                pe.wait_ge(bm_cp, 4)
                for t in range(T):
                    if t > 1:
                        pe.wait_ge(qkv_ev, 2 * (t - 1))
                    for k in range(2):
                        mm = pe.matmul(ps[4 + t % 2][:, 0:384], cqT[:, k, P * t:P * t + P], wq[:, k, :],
                                       start=k == 0, stop=k == 1)
                    mm.then_inc(qkv_ps, 1)
                    pe.matmul(ps[2 + t % 2][:, :], cqT[:, 2, P * t:P * t + P], wkv, start=True, stop=True
                              ).then_inc(qkv_ps, 1)

                def turn_qk(h):
                    pe.wait_ge(stg, h + 1)
                    if h > 0:
                        pe.wait_ge(q_sb, h)
                        pe.wait_ge(k_sb, h)
                    d = DQK[h]
                    for n, (src, bank) in enumerate(((qn, 0), (kn, 1))):
                        for t in range(T):
                            tr = pe.transpose(ps[bank][0:d, P * t:P * t + P], src[:, h % 2, DQ * t:DQ * t + d], ident)
                    tr.then_inc(qk_ps, 1)

                def scores(n):
                    h, t = n // T, n % T
                    d = DQK[h]
                    if t == 0:
                        pe.wait_ge(q_sb, h + 1)
                        pe.wait_ge(k_sb, h + 1)
                    if n >= 2:
                        pe.wait_ge(s_sb, n - 1)
                    pe.matmul(ps[2 + n % 2][:, 0:P * (t + 1)], qT[0:d, h % 2, P * t:P * t + P],
                              kT[0:d, h % 2, 0:P * (t + 1)], start=True, stop=True).then_inc(s_ps, 1)

                def turn_p(n):
                    t = n % T
                    pe.wait_ge(p_dn, n + 1)
                    if n >= 2:
                        pe.wait_ge(pt_ev, n - 1)
                    for k in range(t + 1):
                        tr = pe.transpose(ps[4 + n % 2][:, P * k:P * k + P], psb[:, n % 2, P * k:P * k + P], ident)
                    tr.then_inc(pt_ps, 1)

                def pv(n):
                    h, t = n // T, n % T
                    pe.wait_ge(pt_ev, n + 1)
                    if t == 0 and h >= 2:
                        pe.wait_ge(o_dn, h - 1)
                    for k in range(t + 1):
                        v = kv[:, k, 128 * h + DN:128 * h + DN + DV] if h < MH else \
                            proj[:, k, MV0 + HP * (h - MH):MV0 + HP * (h - MH) + HP]
                        mm = pe.matmul(ps[6 + h % 2][:, DV * t:DV * t + DV], pT[:, n % 2, P * k:P * k + P], v,
                                       start=k == 0, stop=k == t)
                    mm.then_inc(pv_ps, 1)

                pe.wait_ge(h_dn, 3)
                for b in range(6, 10):
                    ada(b)
                pe.wait_ge(qkv_ev, 2 * T)
                pe.wait_ge(ada_ev, 10)
                turn_qk(0)
                scores(0)
                for n in range(8 * T):
                    if n % T == 1 and n // T + 1 < 8:
                        turn_qk(n // T + 1)
                    if n + 1 < 8 * T:
                        scores(n + 1)
                    turn_p(n)
                    if n > 0:
                        pv(n - 1)
                pv(8 * T - 1)

                pe.wait_ge(q_sb, 8)
                pe.wait_ge(k_sb, 8)
                ada(10)
                pe.wait_ge(yn, 1)
                for j in range(KD):
                    if j >= 2:
                        pe.wait_ge(yc_ev, j - 1)
                    for t in range(T):
                        tr = pe.transpose(ps[2 + j % 2][:, P * t:P * t + P],
                                          proj[:, t, y_col[j]:y_col[j] + P], ident)
                    tr.then_inc(yc_ps, 1)
                pe.wait_ge(yc_ev, KD)
                w_o = [slot_of("out", b).rearrange("p (k n) -> p k n", k=KD) for b in range(2)]
                for t in range(T):
                    for b in range(2):
                        w = w_o[b]
                        n = group_no[("out", b, t)]
                        bank_free(n)
                        for k in range(KD):
                            mm = pe.matmul(ps[n % 2][:, :], actT[:, k, P * t:P * t + P], w[:, k, :],
                                           start=k == 0, stop=k == KD - 1)
                        mm.then_inc(acc_ps, 1)

                ada(11)

                def router(t):
                    for k in range(KD):
                        mm = pe.matmul(ps[4][:, NE * t:NE * t + NE], actT[:, k, P * t:P * t + P], rw[:, k, :],
                                       start=k == 0, stop=k == KD - 1)
                    return mm

                to_columns(T, router)
                pe.wait_ge(h_ev, 4 * T)
                router(T - 1).then_inc(rt_ps, 1)
                pe.wait_ge(both_dn, 1)
                for t in range(T):
                    for tt in range(t + 1):
                        pe.matmul(ps[5][:, NE * t:NE * t + NE], stri if tt == t else ones,
                                  both[:, NE * tt:NE * tt + NE], start=tt == 0, stop=tt == t)
                for t in range(T):
                    mm = pe.matmul(ps[6][0:NE, 0:1], both[:, NE * t:NE * t + NE], ones[:, 0:1],
                                   start=t == 0, stop=t == T - 1)
                mm.then_inc(rk_ps, 1)
                pe.wait_ge(ov_dn, 1)
                pe.matmul(ps[7][:, 0:33], ov[0:NE, :].to_broadcast([NE, P]), cst[0:NE, C_UP:C_UP + 33],
                          start=True, stop=True).then_inc(ovb_ps, 1)
                pe.wait_ge(sel_dn, 2 * T)
                for m in range(2 * T):
                    mm = pe.matmul(ps[3][:, 0:NT], row_oh[:, m, :], tile_tok[:, m, :], start=m == 0, stop=m == 2 * T - 1)
                mm.then_inc(tab_ps, 1)
                pe.wait_ge(ada_ev, 12)
                pe.wait_ge(pos_dn, 2)

                def turn_x(e, odd):
                    pe.wait_ge(gat[odd], 8 * (e + 1) if odd else 8 * (e + 2))
                    for j in range(2):
                        for k in range(4):
                            tr = pe.transpose(ps[2 + j][:, P * k:P * k + P],
                                              xg[:, odd, P * (4 * j + k):P * (4 * j + k) + P], ident)
                        tr.then_inc(xt_ps, 1)

                def gate_up(e, odd, first=False):
                    pe.wait_ge(xl_dn, 2 * e + 2)
                    if not first:
                        pe.wait_ge(hid_dn, e)
                    for j in range(2):
                        pe.wait_ge(w_lo, 4 * e + (2 + 2 * j))
                        w = slots_r[3 * odd + j].rearrange("p (k n) -> p k n", k=KD)
                        for k in range(KD):
                            hi, lo, xh, xl = hi_chunk(j, k), w[:, k, :], xeT_r[:, k, :], xeL[:, k, :]
                            pe.matmul(ps[j][:, :], xl, hi, start=k == 0, stop=False)
                            pe.matmul(ps[j][:, :], xh, lo, start=False, stop=False)
                            mm = pe.matmul(ps[j][:, :], xh, hi, start=False, stop=k == KD - 1)
                        mm.then_inc(gu_ps, 1)

                def turn_h(e):
                    pe.wait_ge(hid_dn, e + 1)
                    for k in range(4):
                        tr = pe.transpose(ps[4][:, P * k:P * k + P], hid[:, P * k:P * k + P], ident)
                    tr.then_inc(ht_ps, 1)

                def down(e, odd, first=False):
                    n = 3 * odd + 2
                    pe.wait_ge(ht_ev, e + 1)
                    if not first:
                        pe.wait_ge(y_ev, 2 * e)
                    pe.wait_ge(*expert_loaded(e, odd, 2))
                    w = slots[n].rearrange("p (k n) -> p k n", k=4)
                    for b in range(2):
                        for k in range(4):
                            mm = pe.matmul(ps[6 + b][:, :], hT[:, k, :], w[:, k, 512 * b:512 * b + 512],
                                           start=k == 0, stop=k == 3)
                        mm.then_inc(y_ps, 1)

                turn_x(0, 0)
                gate_up(0, 0, first=True)
                turn_x(1, 1)
                turn_h(0)
                gate_up(1, 1)
                turn_x(2, 0)
                down(0, 0, first=True)
                turn_h(1)
                with pe.Fori(0, NE // 2 - 1) as i:
                    for u_ in range(2):
                        e = 2 * i + (2 + u_)
                        gate_up(e, u_)
                        if u_ == 0:
                            turn_x(e + 1, 1)
                        else:
                            turn_x(e + 1, 0)
                        down(e - 1, 1 - u_)
                        turn_h(e)
                down(NE - 1, 1)

                nov = pe.value_load(ctl[0:1, 0:1], min_val=0, max_val=NOV)
                with pe.Fori(0, NOV) as i:
                    with pe.If(nov > i):
                        pe.wait_ge(ov_g, 16 * i + 16)
                        for j in range(2):
                            for k in range(4):
                                tr = pe.transpose(ps[2 + j][:, P * k:P * k + P],
                                                  xg[:, 1, P * (4 * j + k):P * (4 * j + k) + P], ident)
                        tr.then_inc(ov_xp, 1)
                        pe.wait_ge(ov_xe, i + 1)
                        pe.wait_ge(ov_w, 48 * i + 48)
                        for j in range(2):
                            w = slots[j].rearrange("p (k n) -> p k n", k=KD)
                            for k in range(KD):
                                mm = pe.matmul(ps[j][:, :], xeT[:, k, :], w[:, k, :], start=k == 0, stop=k == KD - 1)
                        mm.then_inc(ov_gu, 1)
                        pe.wait_ge(ov_hd, i + 1)
                        for k in range(4):
                            tr = pe.transpose(ps[4][:, P * k:P * k + P], hid[:, P * k:P * k + P], ident)
                        tr.then_inc(ov_hp, 1)
                        pe.wait_ge(ov_he, i + 1)
                        w = slots[2].rearrange("p (k n) -> p k n", k=4)
                        for b in range(2):
                            for k in range(4):
                                mm = pe.matmul(ps[6 + b][:, :], hT[:, k, :], w[:, k, 512 * b:512 * b + 512],
                                               start=k == 0, stop=k == 3)
                        mm.then_inc(ov_yp, 1)

            @block.scalar
            def _(a):
                step = Counted(a, ach)

                def rstd(dst, src, width, *incs):
                    step(a.activation(dst, src, ACT.Ln, bias=epsc, scale=1.0 / width))
                    return a.activation(dst, dst, ACT.Exp, scale=-0.5)

                def x_rstd(after_w_out):
                    for t in range(T):
                        if after_w_out:
                            a.wait_ge(wo_ev, 2 * t + 2)
                        step(a.activation(hrow[:, 1, :], x[:, t, :], ACT.Square, accum_out=ss_x[:, t:t + 1]))
                    rstd(rs_x, ss_x, D).then_inc(xss, 1)

                def columns_out(base):
                    for t in range(T):
                        for j in range(2):
                            n = 2 * (base + t) + j
                            a.wait_ge(h_ps, n + 1)
                            a.activation(actT[:, 4 * j:4 * j + 4, P * t:P * t + P],
                                         ps[2 + j][:, :].rearrange("p (k n) -> p k n", k=4), ACT.Copy).then_inc(h_ev, 1)

                x_rstd(False)
                a.wait_ge(pcol_ps, 1)
                a.activation(pcol[:], ps[2][:, 0:64], ACT.Copy).then_inc(pcol_sb, 1)
                columns_out(0)
                a.wait_ge(pads, 2)
                a.wait_ge(ach, step.n)

                def conv_silu(f):
                    a.wait_ge(conv_dn, f + 1)
                    a.activation(xbcT[:, f, 3:3 + S], yt[:, f % 2, :], ACT.Silu).then_inc(silu_dn, 1)

                m = 0
                for b in (1, 2, 3, 0, 4, 5):
                    for t in range(T):
                        n = group_no[("in", b, t)]
                        a.wait_ge(acc_ps, n + 1)
                        if b in (1, 2):
                            dst = xbcT[:, 4 * (b - 1) + t, 3:3 + S]
                        elif b == 0:
                            dst = proj[:, t, 0:512]
                        else:
                            c0 = 512 * b - 1024
                            dst = proj[:, t, c0:c0 + in_width[b]]
                        a.activation(dst, ps[n % 2][:, 0:in_width[b]], ACT.Silu if b == 0 else ACT.Copy
                                     ).then_inc(win_ev, 1)
                        if 1 <= m <= 8:
                            conv_silu(m - 1)
                        m += 1
                a.wait_ge(sp_u, 1)
                a.activation(ex, au, ACT.Exp, scale=-1.0).then_inc(sp_e, 1)
                a.wait_ge(par, 14 * 16)
                a.activation(ealog, hpar[:, 1, :], ACT.Exp).then_inc(sp_e, 1)
                a.wait_ge(sp_y, 1)
                a.activation(lny, y1, ACT.Ln).then_inc(sp_l, 1)
                a.wait_ge(win_ev, 24)
                for t in range(T):
                    step(a.activation(sq[:, 0:256], proj[:, t, CQ0:CQ0 + 256], ACT.Square, accum_out=ss_c[:, t:t + 1]))
                    step(a.activation(sq[:, 0:128], proj[:, t, CKV0:CKV0 + 128], ACT.Square,
                                      accum_out=ss_c[:, 4 + t:5 + t]))
                step(rstd(rs_c[:, 0:4], ss_c[:, 0:4], 256))
                rstd(rs_c[:, 4:8], ss_c[:, 4:8], 128).then_inc(c_ss, 1)
                a.wait_ge(cum_ps, 1)
                a.activation(cums, ps[2][:, 0:64], ACT.Copy).then_inc(cum_sb, 1)
                a.wait_ge(cum_sb, 1)
                a.activation(eac, acs, ACT.Exp).then_inc(cume, 1)
                a.activation(cd, tot, ACT.Exp).then_inc(cume, 1)
                a.wait_ge(tend_d, 1)
                a.activation(tend, tend, ACT.Exp).then_inc(cume, 1)
                a.wait_ge(c_ss, 1)
                for c in range(T):
                    a.wait_ge(xs_ps, c + 1)
                    if c >= 2:
                        a.wait_ge(xd_dn, c - 1)
                        a.wait_ge(xde_dn, c - 1)
                    a.activation(xs[:, c % 2, :], ps[2][:, :], ACT.Copy).then_inc(xs_cp, 1)
                    a.wait_ge(bm_ps, c + 1)
                    if c >= 2:
                        a.wait_ge(m_dn, 2 * (c - 1))
                        a.wait_ge(st_ps, c - 1)
                    a.activation(bmcb[:, c % 2, :], ps[3][:, :], ACT.Copy).then_inc(bm_cp, 1)
                    for g in range(2):
                        a.wait_ge(seg_dn, 2 * c + g + 1)
                        a.activation(seg[:, g, :], seg[:, g, :], ACT.Exp).then_inc(seg_ex, 1)
                    a.wait_ge(y_dn, c + 1)
                    for g in range(2):
                        a.activation(xde[:, c % 2, 256 * g:256 * g + 256], proj[:, c, 256 * g:256 * g + 256], ACT.Square,
                                     accum_out=ss_y[:, 2 * c + g:2 * c + g + 1]).then_inc(ysq, 1)
                a.wait_ge(ysq, 8)
                rstd(rs_y[:, 0:8], ss_y[:, 0:8], 256).then_inc(yrs, 1)
                for t in range(T):
                    a.wait_ge(qkv_ps, 2 * t + 1)
                    a.activation(qrow[:, t, :], ps[4 + t % 2][:, 0:384], ACT.Copy).then_inc(qkv_ev, 1)
                    a.wait_ge(qkv_ps, 2 * t + 2)
                    a.activation(kv[:, t, :], ps[2 + t % 2][:, :], ACT.Copy).then_inc(qkv_ev, 1)
                a.wait_ge(hss, 1)
                step(rstd(rs_h[:, 0:32], ss_h[:, 0:32], DQ))
                rstd(rs_h[:, 32:64], ss_h[:, 32:64], HP).then_inc(hrs, 1)

                def k_out(h):
                    d = DQK[h]
                    a.wait_ge(qk_ps, h + 1)
                    if h >= 2:
                        a.wait_ge(s_ps, T * (h - 1))
                    a.activation(kT[0:d, h % 2, :], ps[1][0:d, :], ACT.Copy,
                                 scale=pcol[0:d, (52 if h < MH else 54):(53 if h < MH else 55)]).then_inc(k_sb, 1)

                def expo(n):
                    t = n % T
                    w = P * (t + 1)
                    a.wait_ge(s_sb, n + 1)
                    if n >= 2:
                        a.wait_ge(pt_ps, n - 1)
                    if t == 0 and n >= 2 * T:
                        a.wait_ge(o_dn, n // T - 1)
                    a.activation(psb[:, n % 2, 0:w], ssb[:, n % 2, 0:w], ACT.Exp, scale=-1.0, bias=mx[:, n % 8:n % 8 + 1],
                                 accum_out=lsum[:, n % 8:n % 8 + 1]).then_inc(p_dn, 1)

                def pt_out(n):
                    t = n % T
                    w = P * (t + 1)
                    a.wait_ge(pt_ps, n + 1)
                    if n >= 2:
                        a.wait_ge(pv_ps, n - 1)
                    a.activation(pT[:, n % 2, 0:w], ps[4 + n % 2][:, 0:w], ACT.Copy).then_inc(pt_ev, 1)

                k_out(0)
                for n in range(8 * T):
                    expo(n)
                    if n > 0:
                        pt_out(n - 1)
                    if n % T == 1 and n // T + 1 < 8:
                        k_out(n // T + 1)
                pt_out(8 * T - 1)
                a.wait_ge(o_dn, 8)
                a.wait_ge(p_dn, 8 * T)
                for t in range(T):
                    for j, c0 in enumerate((CQ0, MQ0)):
                        step(a.activation(ssb[:, 0, 0:256], proj[:, t, c0:c0 + 256], ACT.Square,
                                          accum_out=ss_y[:, 8 + 4 * j + t:9 + 4 * j + t]))
                rstd(rs_y[:, 8:16], ss_y[:, 8:16], 256).then_inc(yss, 1)
                x_rstd(True)
                columns_out(T)
                a.wait_ge(rt_ps, 1)
                a.activation(sc, ps[4][:, 0:64], ACT.Exp, scale=-1.0).then_inc(rt_ex, 1)

                def x_out(e):
                    for j in range(2):
                        a.wait_ge(xt_ps, 2 * e + (1 + j))
                        a.activation(xeT_r[:, 4 * j:4 * j + 4, :],
                                     ps[2 + j][:, :].rearrange("p (k n) -> p k n", k=4), ACT.Copy).then_inc(xt_ev, 1)

                def weights_hi(e, odd, j, first=False):
                    a.wait_ge(*expert_loaded(e, odd, j))
                    if not first:
                        a.wait_ge(gu_ps, 2 * e - (1 - j))
                    for jj, k0, k1, buf in hi_parts:
                        if jj == j:
                            if first and buf is hi_parts[3][3]:
                                a.wait_ge(tab_ps, 1)
                            a.activation(buf, slots[3 * odd + j][:, 512 * k0:512 * k1], ACT.Copy
                                         ).then_inc(w_hi, 1)

                def silu(e, first=False):
                    a.wait_ge(gu_ps, 2 * e + 1)
                    if not first:
                        a.wait_ge(hid_dn, e)
                    a.activation(sg, ps[0][:, :], ACT.Silu).then_inc(sil, 1)

                def h_out(e):
                    a.wait_ge(ht_ps, e + 1)
                    a.activation(hT, ps[4][:, :].rearrange("p (k n) -> p k n", k=4), ACT.Copy).then_inc(ht_ev, 1)

                def expert_turn(e, odd, first=False):
                    silu(e, first)
                    weights_hi(e + 1, 1 - odd, 0)
                    x_out(e + 1)
                    weights_hi(e + 1, 1 - odd, 1)
                    h_out(e)

                a.wait_ge(hrow_dn, 2 * T)
                weights_hi(0, 0, 0, first=True)
                weights_hi(0, 0, 1, first=True)
                x_out(0)
                expert_turn(0, 0, first=True)
                with a.Fori(0, NE // 2 - 1) as i:
                    expert_turn(2 * i + 1, 1)
                    expert_turn(2 * i + 2, 0)
                silu(NE - 1)
                x_out(NE)
                h_out(NE - 1)
                nov = a.value_load(ctl[0:1, 0:1], min_val=0, max_val=NOV)
                with a.Fori(0, NOV) as i:
                    with a.If(nov > i):
                        a.wait_ge(ov_xp, i + 1)
                        a.activation(xeT[:, 0:4, :], ps[2][:, :].rearrange("p (k n) -> p k n", k=4), ACT.Copy)
                        a.activation(xeT[:, 4:8, :], ps[3][:, :].rearrange("p (k n) -> p k n", k=4), ACT.Copy
                                     ).then_inc(ov_xe, 1)
                        a.wait_ge(ov_gu, i + 1)
                        a.activation(sg, ps[0][:, :], ACT.Silu).then_inc(ov_si, 1)
                        a.wait_ge(ov_hp, i + 1)
                        a.activation(hT, ps[4][:, :].rearrange("p (k n) -> p k n", k=4), ACT.Copy).then_inc(ov_he, 1)

            @block.vector
            def _(v):
                step = Counted(v, vch)

                def bc(ap, *shape):
                    return ap.to_broadcast([P, *shape])

                def ada_out(b):
                    n = group_no[("ada", b, 0)]
                    v.wait_ge(acc_ps, n + 1)
                    m_ = mod[:, 512 * b:512 * b + 512]
                    v.tensor_tensor(m_, ps[n % 2][:, :], m_, ALU.add).then_inc(ada_ev, 1)

                v.memset(prow[:], 0.0).then_inc(pads, 1)
                v.wait_ge(modb_ld, 16)
                for b in range(4):
                    ada_out(b)

                def h_rows(base, shift, scale):
                    g_ = mod[:, D * scale:D * scale + D]
                    v.wait_ge(gain_ld, 16 + (16 if base else 0))
                    v.wait_ge(ada_ev, 12 if base else 4)
                    v.scalar_tensor_tensor(g_, g_, 1.0, gain[:], ALU.add, ALU.mult).then_inc(g_used, 1)
                    v.wait_ge(g_used, 2 if base else 1)
                    v.wait_ge(xss, 2 if base else 1)
                    for t in range(T):
                        h_ = h_row(base, t)
                        if t >= 2 and not base:
                            v.wait_ge(h_ps, 2 * (t - 1))
                        step(v.scalar_tensor_tensor(h_, x[:, t, :], rs_x[:, t:t + 1], g_, ALU.mult, ALU.mult))
                        v.tensor_tensor(h_, h_, mod[:, D * shift:D * shift + D], ALU.add).then_inc(hrow_dn, 1)

                h_rows(0, 0, 1)
                v.wait_ge(pcol_sb, 1)
                v.memset(xbcT[:, :, 0:3], 0.0).then_inc(pads, 1)
                v.wait_ge(pads, 2)
                for f in range(8):
                    v.wait_ge(win_ev, f + 1)
                    if f >= 2:
                        v.wait_ge(silu_dn, f - 1)
                    y_ = yt[:, f % 2, :]
                    step(v.tensor_scalar(y_, xbcT[:, f, 3:3 + S], pcol[:, 24 + f:25 + f], pcol[:, 32 + f:33 + f],
                                         ALU.mult, ALU.add))
                    for k in (2, 1, 0):
                        ins = v.scalar_tensor_tensor(y_, xbcT[:, f, k:k + S], pcol[:, 8 * k + f:8 * k + f + 1], y_,
                                                     ALU.mult, ALU.add)
                        if k:
                            step(ins)
                        else:
                            ins.then_inc(conv_dn, 1)
                v.wait_ge(par, 14 * 16)
                v.wait_ge(win_ev, 12)
                u3 = u.rearrange("p (t h) -> p t h", t=T)
                step(v.tensor_tensor(u3, proj[:, :, DT0:DT0 + NH], bc(hpar[:, 0:1, :], T, NH), ALU.add))
                v.scalar_tensor_tensor(au, u, -1.0, u, ALU.mult, ALU.max).then_inc(sp_u, 1)
                v.wait_ge(sp_e, 1)
                v.tensor_scalar(y1, ex, 1.0, None, ALU.add).then_inc(sp_y, 1)
                v.wait_ge(sp_y, 1)
                step(v.scalar_tensor_tensor(r1, y1, -1.0, ex, ALU.add, ALU.subtract))
                step(v.reciprocal(tend, y1))
                step(v.tensor_tensor(r1, r1, tend, ALU.mult))
                v.wait_ge(sp_l, 1)
                step(v.tensor_tensor(lny, lny, r1, ALU.subtract))
                step(v.scalar_tensor_tensor(dt, u, 0.0, lny, ALU.max, ALU.add))
                v.wait_ge(sp_e, 2)
                v.scalar_tensor_tensor(dta.rearrange("p (t h) -> p t h", t=T), dt.rearrange("p (t h) -> p t h", t=T),
                                       -1.0, bc(ealog.unsqueeze(1), T, NH), ALU.mult, ALU.mult).then_inc(dta_dn, 1)
                ada_out(4)
                ada_out(5)
                v.wait_ge(c_ss, 1)
                step(v.tensor_tensor(proj[:, :, CQ0:CQ0 + 256], proj[:, :, CQ0:CQ0 + 256],
                                     bc(rs_c[:, 0:4].unsqueeze(2), T, 256), ALU.mult))
                v.tensor_tensor(proj[:, :, CKV0:CKV0 + 128], proj[:, :, CKV0:CKV0 + 128],
                                bc(rs_c[:, 4:8].unsqueeze(2), T, 128), ALU.mult).then_inc(c_nm, 1)
                v.wait_ge(cum_sb, 1)
                v.tensor_tensor(tend, tot, acs, ALU.subtract).then_inc(tend_d, 1)
                for j in range(3):
                    v.wait_ge(c_ps, j + 1)
                    v.tensor_scalar(cqT[:, j, :], ps[3 + j][:, :], pcol[:, 40 + j:41 + j], None, ALU.mult
                                    ).then_inc(c_ev, 1)
                v.wait_ge(cume, 3)
                for c in range(T):
                    b2 = c % 2
                    dtc = dt[:, 8 * c:8 * c + 8].unsqueeze(2)
                    x3 = xdt[:, b2, :].rearrange("p (h n) -> p h n", h=NH)
                    v.wait_ge(xs_cp, c + 1)
                    if c >= 2:
                        v.wait_ge(yd_ps, c - 1)
                        v.wait_ge(st_ps, c - 1)
                        v.wait_ge(y_dn, c - 1)
                        v.wait_ge(ysq, 2 * (c - 1))
                    step(v.tensor_tensor(x3, xs[:, b2, :].rearrange("p (h n) -> p h n", h=NH), bc(dtc, NH, HP), ALU.mult))
                    v.tensor_tensor(xde[:, b2, :].rearrange("p (h n) -> p h n", h=NH), x3,
                                    bc(tend[:, 8 * c:8 * c + 8].unsqueeze(2), NH, HP), ALU.mult).then_inc(xde_dn, 1)
                    for g in range(2):
                        v.wait_ge(dec_ps, 2 * c + g + 1)
                        if c > 0:
                            v.wait_ge(m_dn, 2 * c)
                        col = 8 * c + 4 * g
                        v.tensor_tensor(seg[:, g, :].rearrange("p (h l) -> p h l", h=4),
                                        ps[4 + g][:, :].rearrange("p (h l) -> p h l", h=4),
                                        bc(acs[:, col:col + 4].unsqueeze(2), 4, P), ALU.subtract).then_inc(seg_dn, 1)
                    v.wait_ge(bm_cp, c + 1)
                    for g in range(2):
                        v.wait_ge(seg_ex, 2 * c + g + 1)
                        if c > 0:
                            v.wait_ge(yd_ps, c)
                        cb = bmcb[:, b2, 256 + P * g:256 + P * g + P].unsqueeze(1)
                        v.tensor_tensor(mt[:, g, :].rearrange("p (h l) -> p h l", h=4),
                                        seg[:, g, :].rearrange("p (h l) -> p h l", h=4), bc(cb, 4, P), ALU.mult
                                        ).then_inc(m_dn, 1)
                    y_ = yt[:, b2, :]
                    y3 = y_.rearrange("p (h n) -> p h n", h=NH)
                    v.wait_ge(xd_dn, c + 1)
                    if c > 0:
                        v.wait_ge(yo_ps, c)
                        step(v.tensor_tensor(y3, ps[7][:, :].rearrange("p (h n) -> p h n", h=NH),
                                             bc(eac[:, 8 * c:8 * c + 8].unsqueeze(2), NH, HP), ALU.mult))
                        step(v.tensor_tensor(y_, y_, xd, ALU.add))
                        v.wait_ge(yd_ps, c + 1)
                        step(v.tensor_tensor(y_, ps[6][:, :], y_, ALU.add))
                    else:
                        v.wait_ge(yd_ps, 1)
                        step(v.tensor_tensor(y_, ps[6][:, :], xd, ALU.add))
                    v.tensor_tensor(proj[:, c, 0:512], y_, proj[:, c, 0:512], ALU.mult).then_inc(y_dn, 1)
                    if c < T - 1:
                        v.wait_ge(st_ps, c + 1)
                        if c == 0:
                            v.tensor_copy(hst, ps[0][:, :]).then_inc(h_dn, 1)
                        else:
                            h3 = hst.rearrange("p (h n) -> p h n", h=NH)
                            v.wait_ge(yo_ps, c)
                            step(v.tensor_tensor(h3, h3, bc(cd[:, 8 * c:8 * c + 8].unsqueeze(2), NH, HP), ALU.mult))
                            v.tensor_tensor(hst, hst, ps[0][:, :], ALU.add).then_inc(h_dn, 1)
                v.wait_ge(y_dn, 4)
                v.wait_ge(yrs, 1)
                for c in range(T):
                    for g in range(2):
                        y_ = proj[:, c, 256 * g:256 * g + 256]
                        step(v.tensor_scalar(y_, y_, rs_y[:, 2 * c + g:2 * c + g + 1], None, ALU.mult))
                ada_out(6)
                ada_out(7)
                v.wait_ge(kr_dn, 1)

                def squares(src, width, col):
                    s_ = sq[:, 0:T * width]
                    step(v.tensor_tensor(s_.rearrange("p (t n) -> p t n", t=T), src, src, ALU.mult))
                    step(v.tensor_reduce(ss_h[:, col:col + 16], s_.rearrange("p (a n) -> p a n", a=16), AX.X, ALU.add))

                v.wait_ge(qkv_ev, 2 * T)
                squares(qrow, 384, 0)
                ada_out(8)
                kno = kv.rearrange("p t (h n) -> p t h n", h=MH)[:, :, :, 0:DN]
                sq3 = sq[:, 0:T * 256].rearrange("p (t h n) -> p t h n", t=T, h=MH)
                step(v.tensor_tensor(sq3, kno, kno, ALU.mult))
                step(v.tensor_reduce(ss_h[:, 16:32], sq[:, 0:T * 256].rearrange("p (a n) -> p a n", a=16), AX.X, ALU.add))
                kr = proj[:, :, KR0:KR0 + DR]
                sq4 = sq[:, 0:T * DR].rearrange("p (t n) -> p t n", t=T)
                step(v.tensor_tensor(sq4, kr, kr, ALU.mult))
                step(v.tensor_reduce(ss_kr, sq4, AX.X, ALU.add))
                ssk = ss_h[:, 16:32].rearrange("p (t h) -> p t h", t=T)
                step(v.tensor_tensor(ssk, ssk, bc(ss_kr.unsqueeze(2), T, MH), ALU.add))
                squares(proj[:, :, MQ0:MQ0 + 256], 256, 32)
                s_ = sq[:, 0:T * 256]
                step(v.tensor_tensor(s_.rearrange("p (t n) -> p t n", t=T), proj[:, :, MK0:MK0 + 256],
                                     proj[:, :, MK0:MK0 + 256], ALU.mult))
                v.tensor_reduce(ss_h[:, 48:64], s_.rearrange("p (a n) -> p a n", a=16), AX.X, ALU.add).then_inc(hss, 1)
                ada_out(9)
                v.wait_ge(hrs, 1)

                def stage(h):
                    if h >= 2:
                        v.wait_ge(qk_ps, h - 1)
                    q3 = qn[:, h % 2, :].rearrange("p (t n) -> p t n", t=T)
                    k3 = kn[:, h % 2, :].rearrange("p (t n) -> p t n", t=T)
                    hh = h % MH
                    c0 = 0 if h < MH else 32
                    rq = rs_h[:, c0:c0 + 16].rearrange("p (t h) -> p t h", t=T)[:, :, hh:hh + 1]
                    rk_ = rs_h[:, c0 + 16:c0 + 32].rearrange("p (t h) -> p t h", t=T)[:, :, hh:hh + 1]
                    if h < MH:
                        step(v.tensor_tensor(q3, qrow[:, :, DQ * hh:DQ * hh + DQ], bc(rq, T, DQ), ALU.mult))
                        step(v.tensor_tensor(k3[:, :, 0:DN], kv[:, :, 128 * hh:128 * hh + DN], bc(rk_, T, DN), ALU.mult))
                        v.tensor_tensor(k3[:, :, DN:DQ], kr, bc(rk_, T, DR), ALU.mult).then_inc(stg, 1)
                    else:
                        step(v.tensor_tensor(q3[:, :, 0:HP], proj[:, :, MQ0 + HP * hh:MQ0 + HP * hh + HP],
                                             bc(rq, T, HP), ALU.mult))
                        v.tensor_tensor(k3[:, :, 0:HP], proj[:, :, MK0 + HP * hh:MK0 + HP * hh + HP],
                                        bc(rk_, T, HP), ALU.mult).then_inc(stg, 1)

                def q_out(h):
                    d = DQK[h]
                    v.wait_ge(qk_ps, h + 1)
                    if h >= 2:
                        v.wait_ge(s_ps, T * (h - 1))
                    v.tensor_scalar(qT[0:d, h % 2, :], ps[0][0:d, :],
                                    pcol[0:d, (51 if h < MH else 53):(52 if h < MH else 54)], float(d) ** -0.5,
                                    ALU.mult, ALU.mult).then_inc(q_sb, 1)

                def biased(n):
                    h, t = n // T, n % T
                    w = P * (t + 1)
                    v.wait_ge(s_ps, n + 1)
                    if n >= 2:
                        v.wait_ge(p_dn, n - 1)
                    b_ = cst[:, C_MASK + S - w:C_MASK + S] if h < MH else biasm[:, h - MH, S - w:S]
                    v.tensor_tensor_reduce(ssb[:, n % 2, 0:w], ps[2 + n % 2][:, 0:w], b_, -1.0, 3.0e38,
                                           ALU.add, ALU.min, mx[:, n % 8:n % 8 + 1]).then_inc(s_sb, 1)

                def head_out(h):
                    v.wait_ge(pv_ps, T * (h + 1))
                    step(v.reciprocal(linv, lsum[:, 4 * (h % 2):4 * (h % 2) + 4]))
                    v.tensor_tensor(proj[:, :, o_col[h]:o_col[h] + DV],
                                    ps[6 + h % 2][:, 0:256].rearrange("p (t n) -> p t n", t=T),
                                    bc(linv.unsqueeze(2), T, DV), ALU.mult).then_inc(o_dn, 1)

                stage(0)
                q_out(0)
                for n in range(8 * T):
                    h, t = n // T, n % T
                    if t == 0 and h + 1 < 8:
                        stage(h + 1)
                    biased(n)
                    if t == 1 and h + 1 < 8:
                        q_out(h + 1)
                    if t == 2 and h > 0:
                        head_out(h - 1)
                head_out(7)
                ada_out(10)
                v.wait_ge(yss, 1)
                v.wait_ge(o_dn, 8)
                step(v.tensor_tensor(proj[:, :, CQ0:CQ0 + 256], proj[:, :, CQ0:CQ0 + 256],
                                     bc(rs_y[:, 8:12].unsqueeze(2), T, 256), ALU.mult))
                v.tensor_tensor(proj[:, :, MQ0:MQ0 + 256], proj[:, :, MQ0:MQ0 + 256],
                                bc(rs_y[:, 12:16].unsqueeze(2), T, 256), ALU.mult).then_inc(yn, 1)
                for j in range(KD):
                    v.wait_ge(yc_ps, j + 1)
                    v.tensor_scalar(actT[:, j, :], ps[2 + j % 2][:, :], pcol[:, 43 + j:44 + j], None, ALU.mult
                                    ).then_inc(yc_ev, 1)
                for t in range(T):
                    for b in range(2):
                        n = 2 * t + b
                        v.wait_ge(acc_ps, group_no[("out", b, t)] + 1)
                        x_ = x[:, t, 512 * b:512 * b + 512]
                        if n >= 2:
                            v.wait_ge(wo_ev, n - 1)
                        step(v.tensor_tensor(ws[:, n % 2, :], ps[group_no[("out", b, t)] % 2][:, :],
                                             mod[:, 2 * D + 512 * b:2 * D + 512 * b + 512],
                                             ALU.mult))
                        v.tensor_tensor(x_, x_, ws[:, n % 2, :], ALU.add).then_inc(wo_ev, 1)
                v.wait_ge(wo_ev, 8)
                ada_out(11)
                h_rows(T, 3, 4)

                def r3(ap, a_):
                    return ap.rearrange("p (a b) -> p a b", a=a_)

                v.wait_ge(rt_ex, 1)
                step(v.tensor_scalar(sc, sc, 1.0, None, ALU.add))
                step(v.reciprocal(sc, sc))
                step(v.tensor_tensor(r3(bi, T), r3(sc, T), bc(rbias[:].unsqueeze(1), T, NE), ALU.add))
                b3 = r3(bi, 16)
                hi2, lo2 = r3(mm2[:, 0:32], 16), r3(mm2[:, 32:64], 16)
                step(v.tensor_tensor(hi2, b3[:, :, 0:2], b3[:, :, 2:4], ALU.max))
                step(v.tensor_tensor(lo2, b3[:, :, 0:2], b3[:, :, 2:4], ALU.min))
                g1, g2, g3 = gs.unsqueeze(2), gw.unsqueeze(2), gsel.unsqueeze(2)
                step(v.tensor_tensor(g1, hi2[:, :, 0:1], hi2[:, :, 1:2], ALU.max))
                step(v.tensor_tensor(g2, hi2[:, :, 0:1], hi2[:, :, 1:2], ALU.min))
                step(v.tensor_tensor(g3, lo2[:, :, 0:1], lo2[:, :, 1:2], ALU.max))
                step(v.tensor_tensor(gw, gw, gsel, ALU.max))
                step(v.tensor_tensor(gs, gs, gw, ALU.add))

                def first_max(dst, src, n, rev, tmp):
                    r_ = red[:, 0:4]
                    s3, t3, d3 = r3(src, T), r3(tmp, T), r3(dst, T)
                    step(v.tensor_reduce(r_, s3, AX.X, ALU.max))
                    step(v.tensor_tensor(t3, s3, bc(r_.unsqueeze(2), T, n), ALU.is_equal))
                    step(v.tensor_tensor(t3, t3, bc(cst[:, rev:rev + n].unsqueeze(1), T, n), ALU.mult))
                    step(v.tensor_reduce(r_, t3, AX.X, ALU.max))
                    step(v.tensor_tensor(d3, t3, bc(r_.unsqueeze(2), T, n), ALU.is_equal))

                first_max(gsel, gs, 4, C_REV4, gw)
                step(v.tensor_scalar(gw, gsel, -NEG, NEG, ALU.mult, ALU.add))
                step(v.tensor_tensor(r3(mb, 16), b3, bc(gsel.unsqueeze(2), 16, 4), ALU.mult))
                step(v.tensor_tensor(r3(mb, 16), r3(mb, 16), bc(gw.unsqueeze(2), 16, 4), ALU.add))
                first_max(oh1, mb, NE, C_REV16, eqw)
                step(v.scalar_tensor_tensor(mb, oh1, 100 * NEG, mb, ALU.mult, ALU.add))
                first_max(oh2, mb, NE, C_REV16, eqw)
                v.tensor_tensor(both, oh1, oh2, ALU.add).then_inc(both_dn, 1)


                def of_choice(dst, src):
                    step(v.tensor_tensor(oh_v, oh12, bc(src.unsqueeze(1), 2, T * NE), ALU.mult))
                    return v.tensor_reduce(dst.rearrange("p a t -> p (a t)"),
                                           oh_v.rearrange("p a (t e) -> p (a t) e", t=T), AX.X, ALU.add)

                step(of_choice(w12, sc))
                step(v.tensor_tensor(wsum, w12[:, 0, :], w12[:, 1, :], ALU.add))
                step(v.reciprocal(wsum, wsum))
                step(v.tensor_tensor(w12, w12, bc(wsum.unsqueeze(1), 2, T), ALU.mult))
                v.wait_ge(rk_ps, 1)
                c_, o_ = ps[6][0:NE, 0:1], ov[0:NE, :]
                step(v.tensor_scalar(o_, c_, float(P), None, ALU.is_gt))
                step(v.scalar_tensor_tensor(o_, c_, float(2 * P), o_, ALU.is_gt, ALU.add))
                v.scalar_tensor_tensor(o_, c_, float(3 * P), o_, ALU.is_gt, ALU.add).then_inc(ov_dn, 1)
                step(v.tensor_copy(tmpr, ps[5][:, 0:64]))
                step(v.tensor_scalar(jt, tmpr, float(P), None, ALU.is_ge))
                step(v.tensor_copy(tmps, jt))
                step(v.scalar_tensor_tensor(jt, tmpr, float(2 * P), jt, ALU.is_ge, ALU.add))
                step(v.scalar_tensor_tensor(jt, tmpr, float(3 * P), jt, ALU.is_ge, ALU.add))
                step(v.scalar_tensor_tensor(rowf, jt, float(-P), tmpr, ALU.mult, ALU.add))
                step(of_choice(rf, rowf))
                step(v.tensor_tensor(r3(tilef, T), r3(jt, T), bc(cst[:, C_IOTA16:C_IOTA16 + NE].unsqueeze(1), T, NE),
                                     ALU.add))
                v.wait_ge(ovb_ps, 1)
                step(v.tensor_copy(ovb, ps[7][:, 0:33]))
                step(v.scalar_tensor_tensor(c1, ovb[:, 0:16], float(NE - 1), cst[:, C_IOTA16:C_IOTA16 + NE],
                                            ALU.add, ALU.subtract))
                step(v.tensor_tensor(r3(tmps, T), r3(tmps, T), bc(c1.unsqueeze(1), T, NE), ALU.mult))
                step(v.tensor_tensor(tilef, tilef, tmps, ALU.add))
                step(of_choice(tf, tilef))
                for j in range(2):
                    for t in range(T):
                        m = T * j + t
                        v.tensor_scalar(row_oh[:, m, :], cst[:, C_IOTA:C_IOTA + P], rf[:, j, t:t + 1], None, ALU.is_equal)
                        v.tensor_scalar(tile_tok[:, m, :], cst[:, C_IOTA:C_IOTA + NT], tf[:, j, t:t + 1],
                                        cst[:, C_TOK + t:C_TOK + t + 1], ALU.is_equal, ALU.mult).then_inc(sel_dn, 1)
                step(v.scalar_tensor_tensor(pf, rf, float(NT), tf, ALU.mult, ALU.add))
                v.tensor_copy(pos_i[:], pf).then_inc(pos_dn, 1)
                v.wait_ge(tab_ps, 1)
                v.tensor_copy(slot_idx[:], ps[3][:, 0:NT]).then_inc(tab_sb, 1)
                e7 = r3(cmp7[0:1, :], NOV)
                step(v.tensor_tensor(e7, ovb[0:1, 17:33].unsqueeze(1).to_broadcast([1, NOV, NE]),
                                     cst[0:1, C_IOTA7:C_IOTA7 + NOV].unsqueeze(2).to_broadcast([1, NOV, NE]), ALU.is_le))
                step(v.tensor_reduce(ctf[0:1, 1:8], e7, AX.X, ALU.add))
                step(v.tensor_copy(ctf[0:1, 0:1], ovb[0:1, 16:17]))
                v.tensor_copy(ctl[:], ctf[0:1, 0:8]).then_inc(pos_dn, 1)

                gf = mod[:, 5 * D:6 * D]

                def hidden(e, first=False):
                    v.wait_ge(sil, e + 1)
                    v.wait_ge(gu_ps, 2 * e + 2)
                    if not first:
                        v.wait_ge(ht_ps, e)
                    v.tensor_tensor(hid, ps[1][:, :], sg, ALU.mult).then_inc(hid_dn, 1)

                def y_out(e, odd, first=False):
                    if not first:
                        v.wait_ge(yw[odd], 8 * (e - 1) if odd else 8 * e)
                    for b in range(2):
                        v.wait_ge(y_ps, 2 * e + (1 + b))
                        v.tensor_tensor(ysb[:, odd, 512 * b:512 * b + 512], ps[6 + b][:, :],
                                        gf[:, 512 * b:512 * b + 512], ALU.mult).then_inc(y_ev, 1)

                def x_low(e):
                    for j in range(2):
                        v.wait_ge(xt_ev, 2 * e + (1 + j))
                        v.tensor_tensor(xeL[:, 4 * j:4 * j + 4, :], ps[2 + j][:, :].rearrange("p (k n) -> p k n", k=4),
                                        xeT_r[:, 4 * j:4 * j + 4, :].bitcast(F32),
                                        ALU.subtract).then_inc(xl_dn, 1)

                def weights_lo(e, odd, j):
                    for m, (jj, k0, k1, buf) in enumerate(hi_parts):
                        if jj == j:
                            v.wait_ge(w_hi, 4 * e + (m + 1))
                            v.tensor_tensor(slots_r[3 * odd + j][:, 512 * k0:512 * k1],
                                            slots[3 * odd + j][:, 512 * k0:512 * k1], buf.bitcast(F32), ALU.subtract
                                            ).then_inc(w_lo, 1)

                def expert_turn(e, odd, first=False):
                    weights_lo(e + 1, 1 - odd, 0)
                    hidden(e, first)
                    x_low(e + 1)
                    weights_lo(e + 1, 1 - odd, 1)

                weights_lo(0, 0, 0)
                weights_lo(0, 0, 1)
                x_low(0)
                expert_turn(0, 0, first=True)
                expert_turn(1, 1)
                y_out(0, 0, first=True)
                expert_turn(2, 0)
                y_out(1, 1, first=True)
                expert_turn(3, 1)
                y_out(2, 0)
                with v.Fori(0, NE // 2 - 3) as i:
                    expert_turn(2 * i + 4, 0)
                    y_out(2 * i + 3, 1)
                    expert_turn(2 * i + 5, 1)
                    y_out(2 * i + 4, 0)
                expert_turn(NE - 2, 0)
                y_out(NE - 3, 1)
                hidden(NE - 1)
                y_out(NE - 2, 0)
                y_out(NE - 1, 1)
                v.wait_ge(y_ev, 2 * NE)
                v.wait_ge(pos_dn, 2)
                nov = v.value_load(ctl[0:1, 0:1], min_val=0, max_val=NOV)
                with v.Fori(0, NOV) as i:
                    with v.If(nov > i):
                        v.wait_ge(ov_si, i + 1)
                        v.tensor_tensor(hid, ps[1][:, :], sg, ALU.mult).then_inc(ov_hd, 1)
                        v.wait_ge(ov_yp, i + 1)
                        v.tensor_tensor(ysb[:, 0, 0:512], ps[6][:, :], gf[:, 0:512], ALU.mult)
                        v.tensor_tensor(ysb[:, 0, 512:1024], ps[7][:, :], gf[:, 512:1024], ALU.mult).then_inc(ov_ye, 1)
                for t in range(T):
                    v.wait_ge(cg[t % 2], 32 * (t // 2 + 1))
                    step(v.scalar_tensor_tensor(x[:, t, :], xg[:, t % 2, :], w12[:, 0, t:t + 1], x[:, t, :],
                                                ALU.mult, ALU.add))
                    v.scalar_tensor_tensor(x[:, t, :], ysb[:, t % 2, :], w12[:, 1, t:t + 1], x[:, t, :],
                                           ALU.mult, ALU.add).then_inc(cdn, 1)

            @block.gpsimd
            def _(g):
                step = Counted(g, gch)
                for c in range(T):
                    g.wait_ge(xs_cp, c + 1)
                    if c > 0:
                        g.wait_ge(y_dn, c)
                    else:
                        g.wait_ge(h_ps, 2 * T)
                        g.wait_ge(par, 14 * 16)
                    g.tensor_tensor(xd.rearrange("p (h n) -> p h n", h=NH), xs[:, c % 2, :].rearrange("p (h n) -> p h n", h=NH),
                                    hpar[:, 2, :].unsqueeze(2).to_broadcast([P, NH, HP]), ALU.mult).then_inc(xd_dn, 1)
                cos = cst[:, C_COS:C_COS + 64].rearrange("p (t n) -> p t n", t=T)
                sin = cst[:, C_SIN:C_SIN + 64].rearrange("p (t n) -> p t n", t=T)
                g.wait_ge(y_dn, 4)
                g.wait_ge(qkv_ev, 2 * T)
                for h in range(MH + 1):
                    src = qrow[:, :, DQ * h + DN:DQ * h + DQ] if h < MH else proj[:, :, KR0:KR0 + DR]
                    x1, x2 = src[:, :, 0:16], src[:, :, 16:32]
                    ta, tb, tc, td = (rtmp[:, k, 64 * h:64 * h + 64].rearrange("p (t n) -> p t n", t=T) for k in range(4))
                    g.tensor_tensor(ta, x1, cos, ALU.mult).then_inc(gch, 1)
                    g.tensor_tensor(tb, x2, sin, ALU.mult).then_inc(gch, 1)
                    g.tensor_tensor(tc, x1, sin, ALU.mult).then_inc(gch, 1)
                    g.tensor_tensor(td, x2, cos, ALU.mult).then_inc(gch, 1)
                    step.n += 4
                    g.wait_ge(gch, step.n)
                    step(g.tensor_tensor(x1, ta, tb, ALU.subtract))
                    ins = g.tensor_tensor(x2, tc, td, ALU.add)
                    if h < MH:
                        step(ins)
                    else:
                        ins.then_inc(kr_dn, 1)
                hf = hf_rows.rearrange("(t p) d -> t p d", p=P)
                for t in range(T):
                    g.wait_ge(hrow_dn, T + t + 1)
                    g.dma_start(hf[t], h_row(T, t)).then_inc(hf_wr, 16)
                g.wait_ge(hf_wr, 16 * T)
                g.wait_ge(tab_sb, 1)
                g.wait_ge(xss, 2)

                def gather(dst, col, sem_):
                    g.indirect_dma_start(out=dst, out_offset=None, in_=hf_rows,
                                         in_offset=bass.IndirectOffsetOnAxis(ap=col, axis=0)).then_inc(sem_, 16)

                yv = y_rows.rearrange("(p n) d -> n p d", n=NT)

                for e in range(NE + 4):
                    if e <= NE:
                        if e >= 2:
                            g.wait_ge(xt_ps, 2 * e - 2)
                        gather(xg[:, e % 2, :], slot_idx[:, e:e + 1], gat[e % 2])
                    if e >= 4:
                        g.wait_ge(y_ev, 2 * (e - 4) + 2)
                        g.dma_start(yv[e - 4], ysb[:, e % 2, :]).then_inc(yw[e % 2], 16)
                g.wait_ge(yw[0], 16 * NE // 2)
                g.wait_ge(yw[1], 16 * NE // 2)
                g.wait_ge(pos_dn, 2)
                g.wait_ge(xt_ev, 2 * NE + 2)
                g.memset(turn_mark[:], 0).then_inc(turn, 1)
                nov = g.value_load(ctl[0:1, 0:1], min_val=0, max_val=NOV)
                for i in range(NOV):
                    with g.If(nov > i):
                        gather(xg[:, 1, :], slot_idx[:, NE + i:NE + i + 1], ov_g)
                        g.wait_ge(ov_ye, i + 1)
                        g.dma_start(yv[NE + i], ysb[:, 0, :]).then_inc(ov_yw, 16)
                        g.wait_ge(ov_yw, 16 * i + 16)
                        g.memset(turn_mark[:], 0).then_inc(turn, 1)
                for t in range(T):
                    if t >= 2:
                        g.wait_ge(cdn, t - 1)
                    for j, buf in enumerate((xg, ysb)):
                        g.indirect_dma_start(out=buf[:, t % 2, :], out_offset=None, in_=y_rows,
                                             in_offset=bass.IndirectOffsetOnAxis(ap=pos_i[:, j, t:t + 1], axis=0)
                                             ).then_inc(cg[t % 2], 16)
                g.wait_ge(cg[0], 32 * T // 2)
                g.wait_ge(cg[1], 32 * T // 2)
                g.dma_reset(range(first, last + 1))
        nc.all_engine_barrier(sems_to_clear=range(first, last + 1))

    with nc.Block() as block:
        @block.sync
        def _(sp):
            sp.dma_start(out.rearrange("a (t p) d -> p (a t) d", p=P), x[:]).then_inc(par, 16)
            sp.wait_ge(par, 16)
    ctx.close()


_INS = ["x", "c", "ada_w", "ada_b", "norm_mix_g", "norm_ffn_g", "w_in", "ssd_conv_w", "ssd_conv_b", "ssd_dt_bias",
        "ssd_a_log", "ssd_d", "ssd_norm_g", "mla_q_norm_g", "mla_w_uq", "mla_kv_norm_g", "mla_w_ukv", "mla_q_gain",
        "mla_k_gain", "mla_out_g", "moba_q_gain", "moba_k_gain", "moba_out_g", "rel_bias", "w_out", "router_w",
        "router_bias", "moe_w_gate", "moe_w_up", "moe_w_down"]


def kernel(**inputs):
    import concourse.bacc as _bacc
    from concourse.bass_utils import run_bass_kernel_spmd as _run

    nc = _bacc.Bacc("TRN2", target_bir_lowering=False, num_devices=1)
    arrays, aps = {}, {}
    for name in _INS:
        a = np.ascontiguousarray(inputs[name])
        arrays[f"in_{name}"] = a
        aps[name] = nc.dram_tensor(f"in_{name}", a.shape, mybir.dt.from_np(a.dtype), kind="ExternalInput").ap()
    cpack, bucket_oh = shape_constants()
    arrays["shape_constants"], arrays["bucket_one_hot"] = cpack, bucket_oh
    cp = nc.dram_tensor("shape_constants", cpack.shape, F32, kind="ExternalInput").ap()
    bo = nc.dram_tensor("bucket_one_hot", bucket_oh.shape, F32, kind="ExternalInput").ap()
    out = nc.dram_tensor("out", (1, S, D), F32, kind="ExternalOutput").ap()
    relv = nc.dram_tensor("bias_by_distance", (MH, P, 640), F32, kind="Internal").ap()
    hf_rows = nc.dram_tensor("ffn_rows", (S, D), F32, kind="Internal").ap()
    y_rows = nc.dram_tensor("expert_rows", (P * NT, D), F32, kind="Internal").ap()
    trunk(nc, aps, out, cp, bo, relv, hf_rows, y_rows)
    r = _run(nc, [arrays], core_ids=[0])
    return r.results[0]["out"]
```

```python
from contextlib import ExitStack

import numpy as np

import concourse.bass as bass
from concourse import mybir

F32 = mybir.dt.float32
F32R = mybir.dt.float32r
I32 = mybir.dt.int32
ACT = mybir.ActivationFunctionType
ALU = mybir.AluOpType
AX = mybir.AxisListType

P = 128
S, D, DEPTH = 512, 1024, 2
T = S // P
KD = D // P
NH, HP, NST = 8, 64, 128
NIN = 2728
MH, DQ, DN, DR, DV = 4, 96, 64, 32, 64
NE, DE = 16, 512
NOV = 7
NT = 24
EPS = 1e-6
NEG = -1e30
MAXD = S - 1

Z0, DT0, CQ0, CKV0, KR0, MQ0, MK0, MV0, NPROJ = 0, 512, 520, 776, 904, 936, 1192, 1448, 1704

C_ID, C_TRI, C_NEG, C_STR, C_ONE, C_MASK = 0, 128, 256, 384, 512, 640
C_COS, C_SIN = 1152, 1216
C_EPS, C_REV4, C_REV16, C_IOTA16, C_IOTA7, C_UP = 1280, 1281, 1285, 1301, 1317, 1324
C_IOTA = C_UP + 33
C_TOK = C_IOTA + P
C_HALF = C_TOK + T
C_N = C_HALF + 1


def shape_constants():
    c = np.zeros((P, C_N), np.float32)
    i = np.arange(P)
    c[:, C_ID:C_ID + P] = np.eye(P)
    c[:, C_TRI:C_TRI + P] = i[:, None] <= i[None, :]
    c[:, C_NEG:C_NEG + P] = np.where(i[:, None] <= i[None, :], 0.0, NEG)
    c[:, C_STR:C_STR + P] = i[:, None] < i[None, :]
    c[:, C_ONE:C_ONE + P] = 1.0
    m = np.arange(S)
    c[:, C_MASK:C_MASK + S] = np.where(m[None, :] <= i[:, None] + S - P, 0.0, NEG)
    half = DR // 2
    inv = np.float32(10000.0) ** (np.float32(-2.0) * np.arange(half, dtype=np.float32) / np.float32(DR))
    ang = np.arange(S, dtype=np.float32)[:, None] * inv[None, :].astype(np.float32)
    c[:, C_COS:C_COS + 64] = np.cos(ang).reshape(T, P, half).transpose(1, 0, 2).reshape(P, 64)
    c[:, C_SIN:C_SIN + 64] = np.sin(ang).reshape(T, P, half).transpose(1, 0, 2).reshape(P, 64)
    c[:, C_EPS] = EPS
    c[:, C_REV4:C_REV4 + 4] = 4 - np.arange(4)
    c[:, C_REV16:C_REV16 + 16] = 16 - np.arange(16)
    c[:, C_IOTA16:C_IOTA16 + 16] = np.arange(16)
    c[:, C_IOTA7:C_IOTA7 + 7] = np.arange(7)
    c[:, C_IOTA:C_IOTA + P] = np.arange(P)
    c[:, C_HALF] = -0.5
    c[:, C_TOK:C_TOK + T] = P * np.arange(T)[None, :] + i[:, None]
    e = np.arange(NE)
    c[:NE, C_UP:C_UP + 16] = e[:, None] < e[None, :]
    c[:NE, C_UP + 16] = 1.0
    c[:NE, C_UP + 17:C_UP + 33] = e[:, None] <= e[None, :]
    dist = MAXD - np.arange(640)
    n = np.maximum(dist, 0)
    large = 16 + (np.log(np.maximum(n, 16).astype(np.float32) / np.float32(16))
                  / np.float32(np.log(8.0)) * np.float32(16)).astype(np.int32)
    bucket = np.where(n < 16, n, np.minimum(large, 31))
    oh = np.zeros((33, 640 + 4), np.float32)
    oh[bucket[dist >= 0], np.arange(640)[dist >= 0]] = 1.0
    oh[32, :640][dist < 0] = 1.0
    oh[32, 640:] = NEG
    return c, oh


class Counted:

    def __init__(self, eng, sem):
        self.eng, self.sem, self.n = eng, sem, 0

    def __call__(self, ins):
        ins.then_inc(self.sem, 1)
        self.n += 1
        self.eng.wait_ge(self.sem, self.n)


def trunk(nc, A, out, cpack, bucket_oh, relv, hf_rows, y_rows):
    ctx = ExitStack()

    address = {}

    def sb(name, shape, dt=F32):
        address[name] = -(-nc.sbuf_base // 32) * 32
        return ctx.enter_context(nc.sbuf_tensor(name, shape, dt))

    sems = []

    def sem(name):
        sems.append(ctx.enter_context(nc.semaphore(name)))
        return sems[-1]

    x = sb("x", [P, T, D])
    mod = sb("mod", [P, 6 * D])
    gain = sb("gain", [P, D])
    actT = sb("actT", [P, KD, S])
    cst = sb("cst", [P, C_N])
    biasm = sb("biasm", [P, MH, S])
    rw = sb("rw", [P, KD, NE])
    rbias = sb("rbias", [P, NE])
    csil = sb("csil", [P, KD])
    prow = sb("prow", [64, P])
    pcol = sb("pcol", [P, 64])
    hpar = sb("hpar", [P, 3, NH])
    sml = sb("sml", [P, 1024])
    slot_idx = sb("slot_idx", [P, NT], I32)
    pos_i = sb("pos_i", [P, 2, T], I32)
    ctl = sb("ctl", [1, 1 + NOV], I32)
    turn_mark = sb("turn_mark", [1, 1], I32)
    ring = sb("ring", [P, 3, 4096])
    work = sb("work", [P, 20480])

    mod_r, actT_r, ring_r, work_r = (
        nc.alloc_sbuf_tensor_at(name + "_rounded", shape, F32R, offset=address[name])
        for name, shape in (("mod", [P, 6 * D]), ("actT", [P, KD, S]), ("ring", [P, 3, 4096]), ("work", [P, 20480])))

    def view(off, *dims, of=work):
        n = int(np.prod(dims))
        v = of[:, off:off + n]
        if len(dims) == 2:
            return v.rearrange("p (a b) -> p a b", a=dims[0])
        if len(dims) == 3:
            return v.rearrange("p (a b c) -> p a b c", a=dims[0], b=dims[1])
        return v

    proj = view(0, T, NPROJ)
    XB = 516
    xbcT = view(6816, 8, XB)
    kv = view(6816, T, 512)
    s0 = 10944
    xs = view(s0, 2, 512)
    xdt = view(s0 + 1024, 2, 512)
    xde = view(s0 + 2048, 2, 512)
    bmcb = view(s0 + 3072, 2, 512)
    seg = view(s0 + 4096, 2, 512)
    mt = view(s0 + 5120, 2, 512)
    yt = view(s0 + 6144, 2, 512)
    hst = view(s0 + 7168, 512)
    xd = view(18432 + 1024, 512)
    qn = view(s0, 2, T * DQ)
    kn = view(s0 + 768, 2, T * DQ)
    qT = view(s0 + 1536, 2, 512)
    kT = view(s0 + 2560, 2, 512)
    ssb = view(s0 + 3584, 2, 512)
    psb = view(s0 + 4608, 2, 512)
    pT = view(s0 + 5632, 2, 512)
    sq = view(s0 + 1536, 1536)
    rtmp = view(s0 + 3584, 4, 320)
    hrow = view(18432, 2, D)
    zeros = view(18688, 512)
    hfrow = view(12288, T, D)

    def h_row(base, t):
        return hfrow[:, t, :] if base else hrow[:, t % 2, :]

    ws = view(16384, 2, 512)
    cqT = actT[:, 0:3, :]
    qrow = actT[:, 3:6, :].rearrange("p a b -> p (a b)").rearrange("p (t n) -> p t n", t=T)
    slots = [ring[:, n, :] for n in range(3)] + [view(4096 * n, 4096) for n in range(3)]
    xg = view(12288, 2, D)
    xeT = view(14336, KD, P)
    sg = view(15360, 512)
    hid = view(15872, 512)
    ysb = view(16384, 2, D)
    chosen = view(4096, 2 * T, D)
    hT = view(18432, 4, P)
    xeT_r = view(14336, KD, P, of=work_r)
    xeL = view(18944, KD, P, of=work_r)
    slots_r = [ring_r[:, n, :] for n in range(3)] + [view(4096 * n, 4096, of=work_r) for n in range(3)]
    hi_parts = [(0, 0, 4, mod_r[:, 0:2048]), (0, 4, 8, mod_r[:, 2048:4096]), (1, 0, 2, mod_r[:, 4096:5120]),
                (1, 2, 8, actT_r[:, 2:8, :].rearrange("p a b -> p (a b)"))]

    hL = mod_r[:, 2048:6144].rearrange("p (k n) -> p k n", k=KD)
    in_hi = [view(s0 + 2048 * n, 2048, of=work_r) for n in range(3)] + [mod_r[:, 0:2048]]
    IN_ORDER = (1, 2, 3, 0, 4, 5)
    yL = view(6816, KD, S, of=work_r)
    out_hi = [mod_r[:, 0:2048]] + [view(n, 2048, of=work_r) for n in (17600, 0, 2048)]

    def hi_chunk(j, k):
        _, a0, _, buf = next(h for h in hi_parts if h[0] == j and h[1] <= k < h[2])
        return buf[:, 512 * (k - a0):512 * (k - a0) + 512]


    def sv(off, n):
        return sml[:, off:off + n]

    ss_x, rs_x = sv(0, 4), sv(4, 4)
    u, au, ex, y1, r1, dt, dta = (sv(8 + 32 * k, 32) for k in range(7))
    eac, tend, cd, lny = (sv(264 + 32 * k, 32) for k in range(4))
    cums = sv(740, 64)
    acs, tot = cums[:, 0:32], cums[:, 32:64]
    ealog = sv(392, 8)
    ss_c, rs_c = sv(400, 8), sv(408, 8)
    ss_h, rs_h = sv(416, 64), sv(480, 64)
    ss_y, rs_y = sv(544, 16), sv(560, 16)
    mx, lsum, linv = sv(576, 8), sv(584, 8), sv(592, 4)
    ss_kr = sv(596, 4)
    route = actT[:, 0:2, :].rearrange("p a b -> p (a b)").rearrange("p (k n) -> p k n", k=16)
    sc, bi, mb, oh1, oh2, both, eqw, jt, rowf, tmpr, tmps = (route[:, k, :] for k in range(11))
    oh12 = route[:, 3:5, :]
    oh_v = actT[:, 5, 0:128].rearrange("p (a n) -> p a n", a=2)
    tilef = actT[:, 5, 128:192]
    rt_cols = view(19456, S)[0:NE, :]
    row_oh = actT_r[:, 2:4, :].rearrange("p a b -> p (a b)").rearrange("p (m n) -> p m n", m=2 * T)
    tile_tok = actT_r[:, 4, 0:2 * T * NT].rearrange("p (m n) -> p m n", m=2 * T)
    mm2 = route[:, 11, :]
    gs, gsel, gw = route[:, 12, 0:16], route[:, 12, 16:32], route[:, 12, 32:48]
    red = route[:, 13, :]
    w12 = route[:, 14, 0:8].rearrange("p (a t) -> p a t", a=2)
    wsum, pf = route[:, 14, 8:12], route[:, 14, 16:24].rearrange("p (a t) -> p a t", a=2)
    ov = route[:, 14, 24:25]
    ovb, c1 = route[:, 15, 0:33], route[:, 15, 40:56]
    ctf = route[:, 14, 32:40]
    rf, tf = (route[:, 14, n:n + 8].rearrange("p (a t) -> p a t", a=2) for n in (40, 48))
    cmp7 = sv(624, 112)

    ps = [ctx.enter_context(nc.psum_tensor(f"ps{n}", [P, 512], F32)) for n in range(8)]

    def h_bank(base, t, j):
        return ps[2 + j] if base else ps[2 + 2 * (t % 2) + j]

    ident = cst[:, C_ID:C_ID + P]
    tri = cst[:, C_TRI:C_TRI + P]
    negt = cst[:, C_NEG:C_NEG + P]
    stri = cst[:, C_STR:C_STR + P]
    ones = cst[:, C_ONE:C_ONE + P]
    epsc = cst[:, C_EPS:C_EPS + 1]

    par = sem("small_params_loaded")
    gain_ld = sem("gain_loaded")
    next_ld = [sem(f"next_ada_block{b}_loaded") for b in range(4)]
    next_b = sem("next_ada_bias_loaded")
    next_ps = sem("next_ada_in_psum")
    next_ev = sem("next_ada_block_out")
    modb_ld = sem("mod_bias_loaded")
    bias_ld = sem("attention_bias_loaded")
    zero_wr = sem("further_rows_zeroed")
    slot_ld = [sem(f"slot{n}_loaded") for n in range(6)]
    vch = sem("vector_step")
    ach = sem("scalar_step")
    gch = sem("gpsimd_step")
    acc_ps = sem("acc_in_psum")
    ada_ev = sem("ada_block_out")
    win_ev = sem("w_in_block_out")
    wo_ev = sem("w_out_block_out")
    pcol_ps = sem("params_transposed")
    pcol_sb = sem("params_in_columns")
    xss = sem("x_squares_summed")
    g_used = sem("gain_used")
    hrow_dn = sem("h_row_done")
    h_ps = sem("h_transposed")
    h_ev = sem("h_columns_out")
    pads = sem("conv_pads_zeroed")
    hl_dn = sem("h_columns_low_done")
    in_w_hi = sem("w_in_high_done")
    in_w_lo = sem("w_in_low_done")
    conv_dn = sem("conv_sum_done")
    silu_dn = sem("conv_silu_done")
    sp_u = sem("dt_abs_done")
    sp_e = sem("dt_exp_done")
    sp_y = sem("dt_one_plus_exp_done")
    sp_l = sem("dt_log_done")
    dta_dn = sem("dta_done")
    cum_ps = sem("cumsum_in_psum")
    cum_sb = sem("cumsum_copied")
    tend_d = sem("to_end_difference_done")
    cume = sem("cumsum_exponentials_done")
    c_ss = sem("latent_squares_summed")
    c_nm = sem("latent_normed")
    c_ps = sem("latent_transposed")
    c_ev = sem("latent_columns_out")
    xs_ps = sem("xs_rows_in_psum")
    bm_ps = sem("b_rows_and_cb_in_psum")
    dec_ps = sem("decay_log_in_psum")
    xs_cp = sem("xs_rows_copied")
    bm_cp = sem("b_rows_and_cb_copied")
    xde_dn = sem("xdt_done")
    seg_dn = sem("decay_difference_done")
    seg_ex = sem("decay_exponential_done")
    m_dn = sem("ssd_scores_done")
    yd_ps = sem("y_diag_in_psum")
    yo_ps = sem("y_off_in_psum")
    st_ps = sem("state_in_psum")
    h_dn = sem("state_updated")
    xd_dn = sem("skip_product_done")
    y_dn = sem("ssd_chunk_done")
    ysq = sem("ssd_squares_summed")
    xrs = sem("x_rstd_done")
    crs = sem("latent_rstd_done")
    yrs = sem("mixer_rstd_done")
    hss = sem("head_squares_summed")
    hrs = sem("head_rstd_done")
    qkv_ps = sem("mla_qkv_in_psum")
    qkv_ev = sem("mla_qkv_copied")
    kr_dn = sem("rope_done")
    stg = sem("head_staged")
    qk_ps = sem("qk_transposed")
    q_sb = sem("q_columns_out")
    k_sb = sem("k_columns_out")
    s_ps = sem("scores_in_psum")
    s_sb = sem("scores_biased_and_max")
    p_dn = sem("probs_done")
    pt_ps = sem("probs_transposed")
    pt_ev = sem("probs_columns_out")
    pv_ps = sem("pv_in_psum")
    o_dn = sem("head_output_done")
    yss = sem("mixer_squares_summed")
    yn = sem("mixer_normed")
    yc_ps = sem("mixer_transposed")
    yc_hi = sem("mixer_columns_high_out")
    yc_ev = sem("mixer_columns_out")
    out_w_hi = sem("w_out_high_done")
    out_w_lo = sem("w_out_low_done")
    hf_wr = sem("ffn_rows_stored")
    rt_ps = sem("router_in_psum")
    rt_ex = sem("router_exp_done")
    rt_rows = sem("router_rows_in_psum")
    both_dn = sem("choice_done")
    rk_ps = sem("ranks_in_psum")
    ov_dn = sem("further_tiles_counted")
    ovb_ps = sem("further_tiles_in_psum")
    pos_dn = sem("positions_done")
    sel_dn = sem("slot_selectors_done")
    tab_ps = sem("slot_table_in_psum")
    tab_sb = sem("slot_table_out")
    gat = [sem(f"tokens_gathered{n}") for n in range(2)]
    xt_ps = sem("expert_tokens_transposed")
    xt_ev = sem("expert_tokens_columns_out")
    xl_dn = sem("expert_tokens_low_done")
    w_hi = sem("weights_high_done")
    w_lo = sem("weights_low_done")
    gu_ps = sem("gate_up_in_psum")
    sil = sem("gate_silu_done")
    hid_dn = sem("hidden_done")
    ht_ps = sem("hidden_transposed")
    ht_ev = sem("hidden_columns_out")
    y_ps = sem("expert_out_in_psum")
    y_ev = sem("expert_out_scaled")
    yw = [sem(f"expert_out_stored{n}") for n in range(2)]
    turn = sem("further_tile_turn")
    ov_w = sem("further_weights_loaded")
    ov_g = sem("further_tokens_gathered")
    ov_xp = sem("further_tokens_transposed")
    ov_xe = sem("further_tokens_out")
    ov_gu = sem("further_gate_up_in_psum")
    ov_si = sem("further_silu_done")
    ov_hd = sem("further_hidden_done")
    ov_hp = sem("further_hidden_transposed")
    ov_he = sem("further_hidden_out")
    ov_yp = sem("further_out_in_psum")
    ov_ye = sem("further_out_scaled")
    ov_yw = sem("further_out_stored")
    cg = [sem(f"choices_gathered{n}") for n in range(T)]
    cdn = sem("token_tile_combined")
    first, last = sems[0].num, sems[-1].num
    assert last - first == len(sems) - 1

    def first_ada(sp, layer, b0, b1):
        for b in range(b0, b1):
            if b == 3:
                sp.wait_ge(next_ps, 1)
            src = A["ada_w"][bass.ds(layer, 1), :, 512 * b:512 * b + 512].rearrange("l (k p) n -> p (l k) n", p=P)
            sp.dma_start(slots[b % 3].rearrange("p (k n) -> p k n", k=KD), src).then_inc(next_ld[b], 16)

    def first_ada_bias(sp, layer):
        sp.dma_start(mod[:, 0:2 * D], A["ada_b"][bass.ds(layer, 1), 0:2 * D].broadcast_to([P, 2 * D])).then_inc(next_b, 16)

    def first_ada_sums(pe, banks):
        for b, bank in enumerate(banks):
            pe.wait_ge(next_ld[b], 16)
            w = slots[b % 3].rearrange("p (k n) -> p k n", k=KD)
            for k in range(KD):
                mm = pe.matmul(ps[bank][:, :], csil[:, k:k + 1].to_broadcast([P, P]), w[:, k, :],
                               start=k == 0, stop=k == KD - 1)
            mm.then_inc(next_ps, 1)

    def first_ada_out(v, banks):
        v.wait_ge(next_b, 16)
        for b, bank in enumerate(banks):
            v.wait_ge(next_ps, b + 1)
            m_ = mod[:, 512 * b:512 * b + 512]
            v.tensor_tensor(m_, ps[bank][:, :], m_, ALU.add).then_inc(next_ev, 1)

    with nc.Block() as block:
        @block.sync
        def _(sp):
            sp.dma_start(cst[:], cpack).then_inc(par, 16)
            sp.dma_start(work[0:33, 0:644], bucket_oh).then_inc(par, 16)
            sp.dma_start(sml[0:32, 0:4], A["rel_bias"]).then_inc(gain_ld, 16)
            sp.dma_start(prow[0:KD, :], A["c"].rearrange("a (k p) -> (a k) p", p=P)).then_inc(modb_ld, 16)
            first_ada(sp, 0, 0, 3)
            first_ada_bias(sp, 0)
            sp.dma_start(x[:], A["x"].rearrange("a (t p) d -> p (a t) d", p=P)).then_inc(slot_ld[0], 16)
            sp.dma_start(rw[:], A["router_w"].rearrange("(k p) e -> p k e", p=P)).then_inc(slot_ld[0], 16)
            sp.dma_start(rbias[:], A["router_bias"].rearrange("(a e) -> a e", a=1).broadcast_to([P, NE])
                         ).then_inc(slot_ld[0], 16)
            first_ada(sp, 0, 3, 4)
            sp.wait_ge(ach, 2)
            sp.dma_start(relv, work[0:MH, 1024:1664].unsqueeze(1).to_broadcast([MH, P, 640])).then_inc(slot_ld[1], 16)
            sp.wait_ge(slot_ld[1], 16)
            sp.wait_ge(slot_ld[0], 48)

        @block.tensor
        def _(pe):
            pe.wait_ge(par, 32)
            pe.wait_ge(gain_ld, 16)
            pe.wait_ge(vch, 1)
            pe.matmul(ps[0][0:MH, :], sml[0:33, 0:4], work[0:33, 0:512], start=True, stop=True)
            pe.matmul(ps[1][0:MH, 0:128], sml[0:33, 0:4], work[0:33, 512:640], start=True, stop=True
                      ).then_inc(acc_ps, 1)
            pe.wait_ge(modb_ld, 16)
            pe.transpose(ps[2][:, 0:KD], prow[0:KD, :], cst[0:KD, C_ID:C_ID + KD]).then_inc(acc_ps, 1)
            pe.wait_ge(ach, 3)
            first_ada_sums(pe, (3, 4, 5, 6))

        @block.vector
        def _(v):
            v.wait_ge(par, 32)
            v.tensor_copy(sml[32:33, 0:4], work[32:33, 640:644]).then_inc(vch, 1)
            first_ada_out(v, (3, 4, 5, 6))

        @block.scalar
        def _(a):
            a.wait_ge(acc_ps, 1)
            a.activation(work[0:MH, 1024:1536], ps[0][0:MH, :], ACT.Copy).then_inc(ach, 1)
            a.activation(work[0:MH, 1536:1664], ps[1][0:MH, 0:128], ACT.Copy).then_inc(ach, 1)
            a.wait_ge(acc_ps, 2)
            a.activation(csil[:], ps[2][:, 0:KD], ACT.Silu).then_inc(ach, 1)
    nc.all_engine_barrier(sems_to_clear=range(first, last + 1))

    mixer_loads = [("in", b) for b in IN_ORDER] \
        + [("ada", 4), ("ada", 5), ("mla", 0)] + [("ada", b) for b in range(6, 11)] \
        + [("out", 0), ("out", 1), ("ada", 11)]
    NML = len(mixer_loads)
    last_load = [max(n for n in range(NML) if (n + 1) % 3 == j) for j in range(3)]
    load_no = {what: n for n, what in enumerate(mixer_loads)}
    in_width = [min(512, NIN - 512 * b) for b in range(6)]
    groups = [("in", b, t) for b in IN_ORDER for t in range(T)] \
        + [("ada", b, 0) for b in range(4, 11)] + [("out", b, t) for t in range(T) for b in range(2)] \
        + [("ada", 11, 0)]
    group_no = {g: n for n, g in enumerate(groups)}

    def slot_read(n):
        what, b = mixer_loads[n]
        if what == "mla":
            return qkv_ps, 2 * T
        return acc_ps, 1 + max(m for m, g in enumerate(groups) if g[:2] == (what, b))

    w_in_read = max(m for m, g in enumerate(groups) if g[0] == "in") + 1

    def in_part(b, half):
        n, wd, i = (load_no[("in", b)] + 1) % 3, in_width[b], IN_ORDER.index(b)
        cols = slice(4 * wd * half, 4 * wd * (half + 1))
        return slots[n][:, cols], slots_r[n][:, cols], in_hi[2 * (i % 2) + half][:, 0:4 * wd]

    def out_part(b, half):
        n, cols = (load_no[("out", b)] + 1) % 3, slice(2048 * half, 2048 * (half + 1))
        return slots[n][:, cols], slots_r[n][:, cols], out_hi[2 * b + half]

    def out_loaded(b):
        n = load_no[("out", b)]
        return slot_ld[(n + 1) % 3], 16 * (n // 3 + 1) + (16 if n % 3 == load_no[("mla", 0)] % 3 else 0)

    def in_loaded(b):
        n = load_no[("in", b)]
        return slot_ld[(n + 1) % 3], 16 * (n // 3 + 1)

    def out_before(n, kind):
        return sum(1 for g in groups[:n] if g[0] == kind)

    DQK = [DQ] * MH + [HP] * MH
    o_col = [CQ0 + DV * h for h in range(MH)] + [MQ0 + HP * h for h in range(MH)]
    y_col = [0, 128, 256, 384, CQ0, CQ0 + 128, MQ0, MQ0 + 128]

    base_ld = [16 * (last_load[j] // 3 + 2) + (16 if (load_no[("mla", 0)] + 1) % 3 == j else 0) for j in range(3)]

    def expert_loaded(e, odd, j):
        return slot_ld[3 * odd + j], 8 * (e + 1) if odd else 8 * e + base_ld[j]

    with nc.Fori(0, DEPTH) as L:
        def at_layer(ap, names="a n"):
            return ap[bass.ds(L, 1)]

        with nc.Block() as block:
            @block.sync
            def _(sp):
                def load(what, b, n):
                    slot = slots[(n + 1) % 3]
                    if n >= 3:
                        sp.wait_ge(*slot_read(n - 3))
                    if what == "ada":
                        src = A["ada_w"][bass.ds(L, 1), :, 512 * b:512 * b + 512].rearrange("l (k p) n -> p (l k) n", p=P)
                        dst = slot.rearrange("p (k n) -> p k n", k=KD)
                    elif what == "in":
                        w = in_width[b]
                        src = A["w_in"][bass.ds(L, 1), :, 512 * b:512 * b + w].rearrange("l (k p) n -> p (l k) n", p=P)
                        dst = slot[:, 0:KD * w].rearrange("p (k n) -> p k n", k=KD)
                    elif what == "out":
                        src = A["w_out"][bass.ds(L, 1), :, 512 * b:512 * b + 512].rearrange("l (k p) n -> p (l k) n", p=P)
                        dst = slot.rearrange("p (k n) -> p k n", k=KD)
                    else:
                        src = A["mla_w_uq"][bass.ds(L, 1)].rearrange("l (k p) n -> p (l k) n", p=P)
                        sp.dma_start(slot[:, 0:768].rearrange("p (k n) -> p k n", k=2), src).then_inc(slot_ld[(n + 1) % 3], 16)
                        src = A["mla_w_ukv"][bass.ds(L, 1)].rearrange("l p n -> p (l n)")
                        dst = slot[:, 768:1280]
                    sp.dma_start(dst, src).then_inc(slot_ld[(n + 1) % 3], 16)

                sp.wait_ge(pads, 1)
                rows = [(A["ssd_conv_w"][bass.ds(L, 1)].rearrange("l k (f p) -> (l k f) p", p=P), 0, 32, P),
                        (A["ssd_conv_b"][bass.ds(L, 1)].rearrange("l (f p) -> (l f) p", p=P), 32, 8, P),
                        (A["mla_q_norm_g"][bass.ds(L, 1)].rearrange("l (f p) -> (l f) p", p=P), 40, 2, P),
                        (A["mla_kv_norm_g"][bass.ds(L, 1)].rearrange("l (f p) -> (l f) p", p=P), 42, 1, P),
                        (A["ssd_norm_g"][bass.ds(L, 1)].rearrange("l (f p) -> (l f) p", p=P), 43, 4, P),
                        (A["mla_out_g"][bass.ds(L, 1)].rearrange("l (f p) -> (l f) p", p=P), 47, 2, P),
                        (A["moba_out_g"][bass.ds(L, 1)].rearrange("l (f p) -> (l f) p", p=P), 49, 2, P),
                        (A["mla_q_gain"][bass.ds(L, 1)], 51, 1, DQ), (A["mla_k_gain"][bass.ds(L, 1)], 52, 1, DQ),
                        (A["moba_q_gain"][bass.ds(L, 1)], 53, 1, HP), (A["moba_k_gain"][bass.ds(L, 1)], 54, 1, HP)]
                sp.dma_start(gain[:], A["norm_mix_g"][bass.ds(L, 1)].broadcast_to([P, D])).then_inc(gain_ld, 16)
                load(*mixer_loads[0], 0)
                for src, r0, nr, w in rows:
                    sp.dma_start(prow[r0:r0 + nr, 0:w], src).then_inc(par, 16)
                for n, name in enumerate(("ssd_dt_bias", "ssd_a_log", "ssd_d")):
                    sp.dma_start(hpar[:, n, :], A[name][bass.ds(L, 1)].broadcast_to([P, NH])).then_inc(par, 16)
                load(*mixer_loads[1], 1)
                load(*mixer_loads[2], 2)
                for n, (what, b) in enumerate(mixer_loads):
                    if n == load_no[("mla", 0)]:
                        sp.wait_ge(acc_ps, w_in_read)
                        sp.dma_start(mod[:, 2 * D:], A["ada_b"][bass.ds(L, 1), 2 * D:].broadcast_to([P, 4 * D])
                                     ).then_inc(modb_ld, 16)
                        src = bass.AP(tensor=relv.tensor, offset=relv.offset + P - 1,
                                      ap=[[639, P], [P * 640, MH], [1, S]])
                        sp.dma_start(biasm[:], src).then_inc(bias_ld, 16)
                    if n >= 3:
                        load(what, b, n)
                    if n == load_no[("mla", 0)]:
                        sp.wait_ge(g_used, 1)
                        sp.dma_start(gain[:], A["norm_ffn_g"][bass.ds(L, 1)].broadcast_to([P, D])).then_inc(gain_ld, 16)

                w_gate = A["moe_w_gate"].rearrange("l e (k p) n -> (l e) p k n", p=P)
                w_up = A["moe_w_up"].rearrange("l e (k p) n -> (l e) p k n", p=P)
                w_down = A["moe_w_down"].rearrange("l e (k p) n -> (l e) p k n", p=P)

                def expert(e, odd, wait, parts=(0, 1, 2)):
                    for j in parts:
                        w, k = ((w_gate, KD), (w_up, KD), (w_down, 4))[j]
                        if wait:
                            if j < 2:
                                sp.wait_ge(gu_ps, 2 * (e - 1))
                            else:
                                sp.wait_ge(y_ps, 2 * (e - 1))
                        elif not odd:
                            sp.wait_ge(*slot_read(last_load[j]))
                        n = 3 * odd + j
                        sp.dma_start(slots[n].rearrange("p (k n) -> p k n", k=k),
                                     w[bass.ds(L * NE + e, 1)].rearrange("o p k n -> p (o k) n")
                                     ).then_inc(slot_ld[n], 16)

                expert(0, 0, False, (0, 1))
                sp.wait_ge(wo_ev, 8)
                sp.wait_ge(xss, 2 * T)
                expert(1, 1, False)
                expert(0, 0, False, (2,))
                with sp.Fori(0, NE // 2 - 1) as i:
                    expert(2 * i + 2, 0, True)
                    expert(2 * i + 3, 1, True)
                with sp.If(L < DEPTH - 1):
                    sp.wait_ge(gu_ps, 2 * (NE - 1))
                    first_ada(sp, (L + 1) % DEPTH, 0, 2)
                    sp.wait_ge(y_ps, 2 * (NE - 1))
                    first_ada(sp, (L + 1) % DEPTH, 2, 3)
                    sp.wait_ge(gu_ps, 2 * NE)
                    first_ada_bias(sp, (L + 1) % DEPTH)
                sp.wait_ge(pos_dn, 2)
                nov = sp.value_load(ctl[0:1, 0:1], min_val=0, max_val=NOV)
                with sp.Fori(0, NOV) as i:
                    with sp.If(nov > i):
                        sp.wait_ge(turn, i + 1)
                        eid = sp.value_load(ctl[0:1, bass.ds(i + 1, 1)], min_val=0, max_val=NE - 1)
                        for j, (w, k) in enumerate(((w_gate, KD), (w_up, KD), (w_down, 4))):
                            sp.dma_start(slots[3 + j].rearrange("p (k n) -> p k n", k=k),
                                         w[bass.ds(L * NE + eid, 1)].rearrange("o p k n -> p (o k) n")
                                         ).then_inc(ov_w, 16)
                with sp.If(L < DEPTH - 1):
                    first_ada(sp, (L + 1) % DEPTH, 3, 4)

            @block.tensor
            def _(pe):
                def slot_of(what, b):
                    n = load_no[(what, b)]
                    extra = 16 if n % 3 == load_no[("mla", 0)] % 3 and n >= load_no[("mla", 0)] else 0
                    pe.wait_ge(slot_ld[(n + 1) % 3], 16 * (n // 3 + 1) + extra)
                    return slots[(n + 1) % 3]

                def bank_free(n):
                    if n >= 2:
                        kind = groups[n - 2][0]
                        pe.wait_ge({"ada": ada_ev, "in": win_ev, "out": wo_ev}[kind], out_before(n - 1, kind))

                def ada(b):
                    n = group_no[("ada", b, 0)]
                    w = slot_of("ada", b).rearrange("p (k n) -> p k n", k=KD)
                    bank_free(n)
                    for k in range(KD):
                        mm = pe.matmul(ps[n % 2][:, :], csil[:, k:k + 1].to_broadcast([P, P]), w[:, k, :],
                                       start=k == 0, stop=k == KD - 1)
                        if k == KD - 1:
                            mm.then_inc(acc_ps, 1)


                def to_columns(base, behind=None):
                    for t in range(T):
                        pe.wait_ge(hrow_dn, base + t + 1)
                        if base:
                            pe.wait_ge(h_ev, 2 * (base + t))
                        elif t >= 2:
                            pe.wait_ge(hl_dn, 2 * (t - 1))
                        for j in range(2):
                            for k in range(4):
                                tr = pe.transpose(h_bank(base, t, j)[:, P * k:P * k + P],
                                                  h_row(base, t)[:, P * (4 * j + k):P * (4 * j + k) + P], ident)
                            tr.then_inc(h_ps, 1)
                        if behind is not None and t > 0:
                            behind(t - 1)

                to_columns(0)
                pe.wait_ge(hl_dn, 2 * T)
                pe.wait_ge(par, 14 * 16)
                pe.transpose(ps[2][:, 0:64], prow[:], cst[0:64, C_ID:C_ID + 64]).then_inc(pcol_ps, 1)
                for i, b in enumerate(IN_ORDER):
                    wd = in_width[b]
                    w_parts = [in_part(b, half) for half in range(2)]
                    for t in range(T):
                        n = group_no[("in", b, t)]
                        bank_free(n)
                        for k in range(KD):
                            if t == 0 and k % 4 == 0:
                                pe.wait_ge(in_w_lo, 2 * i + k // 4 + 1)
                            _, lo, hi = (ap.rearrange("p (k n) -> p k n", k=4)[:, k % 4, :] for ap in w_parts[k // 4])
                            hh, hl = actT_r[:, k, :], hL[:, k, :]
                            for m, (w_, h_) in enumerate(((hi, hl), (lo, hh), (hi, hh))):
                                first_, last_ = k == 0 and m == 0, k == KD - 1 and m == 2
                                if b in (1, 2):
                                    mm = pe.matmul(ps[n % 2][:, :], w_[:, P * t:P * t + P], h_, start=first_, stop=last_)
                                else:
                                    mm = pe.matmul(ps[n % 2][:, 0:wd], h_[:, P * t:P * t + P], w_, start=first_, stop=last_)
                        mm.then_inc(acc_ps, 1)
                ada(4)
                ada(5)

                pe.wait_ge(pcol_sb, 1)
                pe.wait_ge(dta_dn, 1)
                pe.matmul(ps[2][:, 0:32], tri, dta, start=True, stop=True)
                pe.matmul(ps[2][:, 32:64], ones, dta, start=True, stop=True).then_inc(cum_ps, 1)
                pe.wait_ge(c_nm, 1)
                for j in range(3):
                    for t in range(T):
                        tr = pe.transpose(ps[3 + j][:, P * t:P * t + P],
                                          proj[:, t, CQ0 + P * j:CQ0 + P * j + P], ident)
                    tr.then_inc(c_ps, 1)
                pe.wait_ge(cume, 3)
                pe.wait_ge(c_ev, 3)
                pe.wait_ge(silu_dn, 8)

                for c in range(T):
                    cs = slice(3 + P * c, 3 + P * c + P)
                    if c > 0:
                        pe.wait_ge(xs_cp, c)
                    for f in range(4):
                        tr = pe.transpose(ps[2][:, P * f:P * f + P], xbcT[:, f, cs], ident)
                    tr.then_inc(xs_ps, 1)
                    if c > 0:
                        pe.wait_ge(bm_cp, c)
                    for g in range(2):
                        pe.transpose(ps[3][:, P * g:P * g + P], xbcT[:, 4 + g, cs], ident)
                    for g in range(2):
                        mm = pe.matmul(ps[3][:, 256 + P * g:256 + P * g + P], xbcT[:, 4 + g, cs], xbcT[:, 6 + g, cs],
                                       start=True, stop=True)
                    mm.then_inc(bm_ps, 1)
                    for g in range(2):
                        if c > 0:
                            pe.wait_ge(seg_dn, 2 * (c - 1) + g + 1)
                        for h in range(4):
                            col = 8 * c + 4 * g + h
                            pe.matmul(ps[4 + g][:, P * h:P * h + P], ident, negt, start=True, stop=False)
                            mm = pe.matmul(ps[4 + g][:, P * h:P * h + P], dta[:, col:col + 1].to_broadcast([P, P]), tri,
                                           start=False, stop=True)
                        mm.then_inc(dec_ps, 1)
                    if c == 0:
                        pe.wait_ge(ada_ev, 2)
                    if c < T - 1:
                        pe.wait_ge(bm_cp, c + 1)
                        pe.wait_ge(xde_dn, c + 1)
                        if c > 0:
                            pe.wait_ge(h_dn, c)
                        for g in range(2):
                            mm = pe.matmul(ps[0][:, 256 * g:256 * g + 256], bmcb[:, c % 2, P * g:P * g + P],
                                           xde[:, c % 2, 256 * g:256 * g + 256], start=True, stop=True)
                        mm.then_inc(st_ps, 1)
                    if c > 0:
                        pe.wait_ge(h_dn, c)
                        pe.wait_ge(y_dn, c)
                        for g in range(2):
                            mm = pe.matmul(ps[7][:, 256 * g:256 * g + 256], xbcT[:, 6 + g, cs],
                                           hst[:, 256 * g:256 * g + 256], start=True, stop=True)
                        mm.then_inc(yo_ps, 1)
                    pe.wait_ge(m_dn, 2 * c + 2)
                    pe.wait_ge(xde_dn, c + 1)
                    for g in range(2):
                        for h in range(4):
                            hh = 4 * g + h
                            mm = pe.matmul(ps[6][:, HP * hh:HP * hh + HP], mt[:, g, P * h:P * h + P],
                                           xdt[:, c % 2, HP * hh:HP * hh + HP], start=True, stop=True)
                    mm.then_inc(yd_ps, 1)

                w = slot_of("mla", 0)
                wq = w[:, 0:768].rearrange("p (k n) -> p k n", k=2)
                wkv = w[:, 768:1280]
                pe.wait_ge(y_dn, 4)
                pe.wait_ge(seg_dn, 8)
                pe.wait_ge(xs_cp, 4)
                pe.wait_ge(bm_cp, 4)
                for t in range(T):
                    if t > 1:
                        pe.wait_ge(qkv_ev, 2 * (t - 1))
                    for k in range(2):
                        mm = pe.matmul(ps[4 + t % 2][:, 0:384], cqT[:, k, P * t:P * t + P], wq[:, k, :],
                                       start=k == 0, stop=k == 1)
                    mm.then_inc(qkv_ps, 1)
                    pe.matmul(ps[2 + t % 2][:, :], cqT[:, 2, P * t:P * t + P], wkv, start=True, stop=True
                              ).then_inc(qkv_ps, 1)

                def turn_qk(h):
                    pe.wait_ge(stg, h + 1)
                    if h > 0:
                        pe.wait_ge(q_sb, h)
                        pe.wait_ge(k_sb, h)
                    d = DQK[h]
                    for n, (src, bank) in enumerate(((qn, 0), (kn, 1))):
                        for t in range(T):
                            tr = pe.transpose(ps[bank][0:d, P * t:P * t + P], src[:, h % 2, DQ * t:DQ * t + d], ident)
                    tr.then_inc(qk_ps, 1)

                def scores(n):
                    h, t = n // T, n % T
                    d = DQK[h]
                    if t == 0:
                        pe.wait_ge(q_sb, h + 1)
                        pe.wait_ge(k_sb, h + 1)
                    if n >= 2:
                        pe.wait_ge(s_sb, n - 1)
                    pe.matmul(ps[2 + n % 2][:, 0:P * (t + 1)], qT[0:d, h % 2, P * t:P * t + P],
                              kT[0:d, h % 2, 0:P * (t + 1)], start=True, stop=True).then_inc(s_ps, 1)

                def turn_p(n):
                    t = n % T
                    pe.wait_ge(p_dn, n + 1)
                    if n >= 2:
                        pe.wait_ge(pt_ev, n - 1)
                    for k in range(t + 1):
                        tr = pe.transpose(ps[4 + n % 2][:, P * k:P * k + P], psb[:, n % 2, P * k:P * k + P], ident)
                    tr.then_inc(pt_ps, 1)

                def pv(n):
                    h, t = n // T, n % T
                    pe.wait_ge(pt_ev, n + 1)
                    if t == 0 and h >= 2:
                        pe.wait_ge(o_dn, h - 1)
                    for k in range(t + 1):
                        v = kv[:, k, 128 * h + DN:128 * h + DN + DV] if h < MH else \
                            proj[:, k, MV0 + HP * (h - MH):MV0 + HP * (h - MH) + HP]
                        mm = pe.matmul(ps[6 + h % 2][:, DV * t:DV * t + DV], pT[:, n % 2, P * k:P * k + P], v,
                                       start=k == 0, stop=k == t)
                    mm.then_inc(pv_ps, 1)

                pe.wait_ge(h_dn, 3)
                for b in range(6, 10):
                    ada(b)
                pe.wait_ge(qkv_ev, 2 * T)
                pe.wait_ge(ada_ev, 6)
                turn_qk(0)
                scores(0)
                scores(1)
                for n in range(8 * T):
                    if n % T == 0 and n // T + 1 < 8:
                        turn_qk(n // T + 1)
                    if n + 2 < 8 * T:
                        scores(n + 2)
                    turn_p(n)
                    if n > 0:
                        pv(n - 1)
                pv(8 * T - 1)

                pe.wait_ge(q_sb, 8)
                pe.wait_ge(k_sb, 8)
                ada(10)
                pe.wait_ge(yn, 1)
                for j in range(KD):
                    if j >= 4:
                        pe.wait_ge(yc_ev, j - 3)
                    for t in range(T):
                        tr = pe.transpose(ps[2 + j % 4][:, P * t:P * t + P],
                                          proj[:, t, y_col[j]:y_col[j] + P], ident)
                    tr.then_inc(yc_ps, 1)
                pe.wait_ge(yc_ev, KD)
                for t in range(T):
                    for b in range(2):
                        n = group_no[("out", b, t)]
                        bank_free(n)
                        for k in range(KD):
                            if t == 0 and k % 4 == 0:
                                pe.wait_ge(out_w_lo, 2 * b + k // 4 + 1)
                            _, lo, hi = (ap.rearrange("p (k n) -> p k n", k=4)[:, k % 4, :] for ap in out_part(b, k // 4))
                            yh, yl = (ap[:, k, P * t:P * t + P] for ap in (actT_r, yL))
                            pe.matmul(ps[n % 2][:, :], yl, hi, start=k == 0, stop=False)
                            pe.matmul(ps[n % 2][:, :], yh, lo, start=False, stop=False)
                            mm = pe.matmul(ps[n % 2][:, :], yh, hi, start=False, stop=k == KD - 1)
                        mm.then_inc(acc_ps, 1)


                def router(t):
                    for k in range(KD):
                        mm = pe.matmul(ps[4][0:NE, P * t:P * t + P], rw[:, k, :], actT[:, k, P * t:P * t + P],
                                       start=k == 0, stop=k == KD - 1)
                    return mm

                to_columns(T, router)
                pe.wait_ge(h_ev, 4 * T)
                router(T - 1).then_inc(rt_ps, 1)
                pe.wait_ge(rt_ex, 1)
                for t in range(T):
                    tr = pe.transpose(ps[5][:, NE * t:NE * t + NE], rt_cols[:, P * t:P * t + P], cst[0:NE, C_ID:C_ID + NE])
                tr.then_inc(rt_rows, 1)
                ada(11)
                pe.wait_ge(both_dn, 1)
                for t in range(T):
                    for tt in range(t + 1):
                        pe.matmul(ps[5][:, NE * t:NE * t + NE], stri if tt == t else ones,
                                  both[:, NE * tt:NE * tt + NE], start=tt == 0, stop=tt == t)
                for t in range(T):
                    mm = pe.matmul(ps[6][0:NE, 0:1], both[:, NE * t:NE * t + NE], ones[:, 0:1],
                                   start=t == 0, stop=t == T - 1)
                mm.then_inc(rk_ps, 1)
                pe.wait_ge(ov_dn, 1)
                pe.matmul(ps[7][:, 0:33], ov[0:NE, :].to_broadcast([NE, P]), cst[0:NE, C_UP:C_UP + 33],
                          start=True, stop=True).then_inc(ovb_ps, 1)
                pe.wait_ge(sel_dn, 2 * T)
                for m in range(2 * T):
                    mm = pe.matmul(ps[3][:, 0:NT], row_oh[:, m, :], tile_tok[:, m, :], start=m == 0, stop=m == 2 * T - 1)
                mm.then_inc(tab_ps, 1)
                pe.wait_ge(ada_ev, 8)
                pe.wait_ge(pos_dn, 2)

                def turn_x(e, odd):
                    pe.wait_ge(gat[odd], 8 * (e + 1) if odd else 8 * (e + 2))
                    for j in range(2):
                        for k in range(4):
                            tr = pe.transpose(ps[2 + j][:, P * k:P * k + P],
                                              xg[:, odd, P * (4 * j + k):P * (4 * j + k) + P], ident)
                        tr.then_inc(xt_ps, 1)

                def gate_up(e, odd, first=False):
                    pe.wait_ge(xl_dn, 2 * e + 2)
                    if not first:
                        pe.wait_ge(hid_dn, e)
                    for j in range(2):
                        pe.wait_ge(w_lo, 4 * e + (2 + 2 * j))
                        w = slots_r[3 * odd + j].rearrange("p (k n) -> p k n", k=KD)
                        for k in range(KD):
                            hi, lo, xh, xl = hi_chunk(j, k), w[:, k, :], xeT_r[:, k, :], xeL[:, k, :]
                            pe.matmul(ps[j][:, :], xl, hi, start=k == 0, stop=False)
                            pe.matmul(ps[j][:, :], xh, lo, start=False, stop=False)
                            mm = pe.matmul(ps[j][:, :], xh, hi, start=False, stop=k == KD - 1)
                        mm.then_inc(gu_ps, 1)

                def turn_h(e):
                    pe.wait_ge(hid_dn, e + 1)
                    for k in range(4):
                        tr = pe.transpose(ps[4][:, P * k:P * k + P], hid[:, P * k:P * k + P], ident)
                    tr.then_inc(ht_ps, 1)

                def down(e, odd, first=False):
                    n = 3 * odd + 2
                    pe.wait_ge(ht_ev, e + 1)
                    if not first:
                        pe.wait_ge(y_ev, 2 * e)
                    pe.wait_ge(*expert_loaded(e, odd, 2))
                    w = slots[n].rearrange("p (k n) -> p k n", k=4)
                    for b in range(2):
                        for k in range(4):
                            mm = pe.matmul(ps[6 + b][:, :], hT[:, k, :], w[:, k, 512 * b:512 * b + 512],
                                           start=k == 0, stop=k == 3)
                        mm.then_inc(y_ps, 1)

                turn_x(0, 0)
                gate_up(0, 0, first=True)
                turn_x(1, 1)
                turn_h(0)
                gate_up(1, 1)
                turn_x(2, 0)
                down(0, 0, first=True)
                turn_h(1)
                with pe.Fori(0, NE // 2 - 1) as i:
                    for u_ in range(2):
                        e = 2 * i + (2 + u_)
                        gate_up(e, u_)
                        if u_ == 0:
                            turn_x(e + 1, 1)
                        else:
                            turn_x(e + 1, 0)
                        down(e - 1, 1 - u_)
                        turn_h(e)
                down(NE - 1, 1)

                nov = pe.value_load(ctl[0:1, 0:1], min_val=0, max_val=NOV)
                with pe.Fori(0, NOV) as i:
                    with pe.If(nov > i):
                        pe.wait_ge(ov_g, 16 * i + 16)
                        for j in range(2):
                            for k in range(4):
                                tr = pe.transpose(ps[2 + j][:, P * k:P * k + P],
                                                  xg[:, 1, P * (4 * j + k):P * (4 * j + k) + P], ident)
                        tr.then_inc(ov_xp, 1)
                        pe.wait_ge(ov_xe, i + 1)
                        pe.wait_ge(ov_w, 48 * i + 48)
                        for j in range(2):
                            w = slots[3 + j].rearrange("p (k n) -> p k n", k=KD)
                            for k in range(KD):
                                mm = pe.matmul(ps[j][:, :], xeT[:, k, :], w[:, k, :], start=k == 0, stop=k == KD - 1)
                        mm.then_inc(ov_gu, 1)
                        pe.wait_ge(ov_hd, i + 1)
                        for k in range(4):
                            tr = pe.transpose(ps[4][:, P * k:P * k + P], hid[:, P * k:P * k + P], ident)
                        tr.then_inc(ov_hp, 1)
                        pe.wait_ge(ov_he, i + 1)
                        w = slots[5].rearrange("p (k n) -> p k n", k=4)
                        for b in range(2):
                            for k in range(4):
                                mm = pe.matmul(ps[6 + b][:, :], hT[:, k, :], w[:, k, 512 * b:512 * b + 512],
                                               start=k == 0, stop=k == 3)
                        mm.then_inc(ov_yp, 1)

                with pe.If(L < DEPTH - 1):
                    pe.wait_ge(hid_dn, NE)
                    pe.wait_ge(xt_ev, 2 * NE + 2)
                    first_ada_sums(pe, (5, 0, 1, 2))

            @block.scalar
            def _(a):
                step = Counted(a, ach)

                def x_squares(after_w_out):
                    for t in range(T):
                        if after_w_out:
                            a.wait_ge(wo_ev, 2 * t + 2)
                        if t:
                            a.wait_ge(xss, t + (T if after_w_out else 0))
                        unused = view(4096, D) if after_w_out else hrow[:, 1, :]
                        a.activation(unused, x[:, t, :], ACT.Square, accum_out=ss_x[:, t:t + 1]).then_inc(xss, 1)

                def in_weights_hi(i):
                    a.wait_ge(*in_loaded(IN_ORDER[i]))
                    for half in range(2):
                        raw, _, hi = in_part(IN_ORDER[i], half)
                        if i == 1 and half == 1:
                            a.wait_ge(hrow_dn, T)
                        a.activation(hi, raw, ACT.Copy).then_inc(in_w_hi, 1)

                def columns_out(base):
                    for t in range(T):
                        if base == 0 and t == 2:
                            in_weights_hi(0)
                        for j in range(2):
                            n = 2 * (base + t) + j
                            a.wait_ge(h_ps, n + 1)
                            a.activation((actT if base else actT_r)[:, 4 * j:4 * j + 4, P * t:P * t + P],
                                         h_bank(base, t, j)[:, :].rearrange("p (k n) -> p k n", k=4), ACT.Copy
                                         ).then_inc(h_ev, 1)

                x_squares(False)
                columns_out(0)
                a.wait_ge(pcol_ps, 1)
                a.activation(pcol[:], ps[2][:, 0:64], ACT.Copy).then_inc(pcol_sb, 1)
                in_weights_hi(1)
                a.wait_ge(pads, 2)
                a.wait_ge(ach, step.n)

                def conv_silu(f):
                    a.wait_ge(conv_dn, f + 1)
                    a.activation(xbcT[:, f, 3:3 + S], yt[:, f % 2, :], ACT.Silu).then_inc(silu_dn, 1)

                m = 0
                for i, b in enumerate(IN_ORDER):
                    for t in range(T):
                        n = group_no[("in", b, t)]
                        a.wait_ge(acc_ps, n + 1)
                        if b in (1, 2):
                            dst = xbcT[:, 4 * (b - 1) + t, 3:3 + S]
                        elif b == 0:
                            dst = proj[:, t, 0:512]
                        else:
                            c0 = 512 * b - 1024
                            dst = proj[:, t, c0:c0 + in_width[b]]
                        a.activation(dst, ps[n % 2][:, 0:in_width[b]], ACT.Silu if b == 0 else ACT.Copy
                                     ).then_inc(win_ev, 1)
                        if 1 <= m <= 8:
                            conv_silu(m - 1)
                        m += 1
                    if i + 2 < len(IN_ORDER):
                        in_weights_hi(i + 2)
                a.wait_ge(sp_u, 1)
                a.activation(ex, au, ACT.Exp, scale=-1.0).then_inc(sp_e, 1)
                a.wait_ge(par, 14 * 16)
                a.activation(ealog, hpar[:, 1, :], ACT.Exp).then_inc(sp_e, 1)
                a.wait_ge(sp_y, 1)
                a.activation(lny, y1, ACT.Ln).then_inc(sp_l, 1)
                a.wait_ge(win_ev, 24)
                for t in range(T):
                    if t:
                        a.wait_ge(c_ss, 2 * t)
                    a.activation(sq[:, 0:256], proj[:, t, CQ0:CQ0 + 256], ACT.Square, accum_out=ss_c[:, t:t + 1]
                                 ).then_inc(c_ss, 1)
                    a.activation(sq[:, 256:384], proj[:, t, CKV0:CKV0 + 128], ACT.Square, accum_out=ss_c[:, 4 + t:5 + t]
                                 ).then_inc(c_ss, 1)
                a.wait_ge(cum_ps, 1)
                a.activation(cums, ps[2][:, 0:64], ACT.Copy).then_inc(cum_sb, 1)
                a.wait_ge(cum_sb, 1)
                a.activation(eac, acs, ACT.Exp).then_inc(cume, 1)
                a.activation(cd, tot, ACT.Exp).then_inc(cume, 1)
                a.wait_ge(tend_d, 1)
                a.activation(tend, tend, ACT.Exp).then_inc(cume, 1)
                a.wait_ge(c_ss, 2 * T)
                for c in range(T):
                    a.wait_ge(xs_ps, c + 1)
                    if c >= 2:
                        a.wait_ge(xd_dn, c - 1)
                        a.wait_ge(xde_dn, c - 1)
                    a.activation(xs[:, c % 2, :], ps[2][:, :], ACT.Copy).then_inc(xs_cp, 1)
                    a.wait_ge(bm_ps, c + 1)
                    if c >= 2:
                        a.wait_ge(m_dn, 2 * (c - 1))
                        a.wait_ge(st_ps, c - 1)
                    a.activation(bmcb[:, c % 2, :], ps[3][:, :], ACT.Copy).then_inc(bm_cp, 1)
                    for g in range(2):
                        a.wait_ge(seg_dn, 2 * c + g + 1)
                        a.activation(seg[:, g, :], seg[:, g, :], ACT.Exp).then_inc(seg_ex, 1)
                    a.wait_ge(y_dn, c + 1)
                    for g in range(2):
                        a.activation(xde[:, c % 2, 256 * g:256 * g + 256], proj[:, c, 256 * g:256 * g + 256], ACT.Square,
                                     accum_out=ss_y[:, 2 * c + g:2 * c + g + 1]).then_inc(ysq, 1)
                for t in range(T):
                    a.wait_ge(qkv_ps, 2 * t + 1)
                    a.activation(qrow[:, t, :], ps[4 + t % 2][:, 0:384], ACT.Copy).then_inc(qkv_ev, 1)
                    a.wait_ge(qkv_ps, 2 * t + 2)
                    a.activation(kv[:, t, :], ps[2 + t % 2][:, :], ACT.Copy).then_inc(qkv_ev, 1)
                a.wait_ge(hss, 1)
                step(a.activation(rs_h[:, 0:32], ss_h[:, 0:32], ACT.Ln, bias=epsc, scale=1.0 / DQ))
                step(a.activation(rs_h[:, 32:64], ss_h[:, 32:64], ACT.Ln, bias=epsc, scale=1.0 / HP))
                a.activation(rs_h, rs_h, ACT.Exp, scale=-0.5).then_inc(hrs, 1)
                def k_out(h):
                    d = DQK[h]
                    a.wait_ge(qk_ps, h + 1)
                    if h >= 2:
                        a.wait_ge(s_ps, T * (h - 1))
                    a.activation(kT[0:d, h % 2, :], ps[1][0:d, :], ACT.Copy,
                                 scale=pcol[0:d, (52 if h < MH else 54):(53 if h < MH else 55)]).then_inc(k_sb, 1)

                def expo(n):
                    t = n % T
                    w = P * (t + 1)
                    a.wait_ge(s_sb, n + 1)
                    if n >= 2:
                        a.wait_ge(pt_ps, n - 1)
                    if t == 0 and n >= 2 * T:
                        a.wait_ge(o_dn, n // T - 1)
                    a.activation(psb[:, n % 2, 0:w], ssb[:, n % 2, 0:w], ACT.Exp, scale=-1.0, bias=mx[:, n % 8:n % 8 + 1],
                                 accum_out=lsum[:, n % 8:n % 8 + 1]).then_inc(p_dn, 1)

                def pt_out(n):
                    t = n % T
                    w = P * (t + 1)
                    a.wait_ge(pt_ps, n + 1)
                    if n >= 2:
                        a.wait_ge(pv_ps, n - 1)
                    a.activation(pT[:, n % 2, 0:w], ps[4 + n % 2][:, 0:w], ACT.Copy).then_inc(pt_ev, 1)

                def out_weights_hi(b, half):
                    if half == 0:
                        a.wait_ge(*out_loaded(b))
                    raw, _, hi = out_part(b, half)
                    a.activation(hi, raw, ACT.Copy).then_inc(out_w_hi, 1)

                k_out(0)
                for n in range(8 * T):
                    if n in (24, 28):
                        a.wait_ge(zero_wr, 16)
                        out_weights_hi(0, (n - 24) // 4)
                    expo(n)
                    if n > 0:
                        pt_out(n - 1)
                    if n % T == 0 and n // T + 1 < 8:
                        k_out(n // T + 1)
                pt_out(8 * T - 1)
                a.wait_ge(o_dn, 8)
                a.wait_ge(p_dn, 8 * T)
                for t in range(T):
                    for j, c0 in enumerate((CQ0, MQ0)):
                        if t:
                            a.wait_ge(yss, 2 * t)
                        a.activation(ssb[:, j, 0:256], proj[:, t, c0:c0 + 256], ACT.Square,
                                     accum_out=ss_y[:, 8 + 4 * j + t:9 + 4 * j + t]).then_inc(yss, 1)
                for j in range(KD):
                    a.wait_ge(yc_ps, j + 1)
                    a.activation(actT_r[:, j, :], ps[2 + j % 4][:, :], ACT.Copy, scale=pcol[:, 43 + j:44 + j]
                                 ).then_inc(yc_hi, 1)
                out_weights_hi(1, 0)
                out_weights_hi(1, 1)
                a.wait_ge(yss, 2 * T)
                x_squares(True)
                def weights_hi(e, odd, parts, first=False):
                    for m in parts:
                        j, k0, k1, buf = hi_parts[m]
                        if m % 2 == 0:
                            a.wait_ge(*expert_loaded(e, odd, j))
                            if not first:
                                a.wait_ge(gu_ps, 2 * e - (1 - j))
                        a.activation(buf, slots[3 * odd + j][:, 512 * k0:512 * k1], ACT.Copy).then_inc(w_hi, 1)

                columns_out(T)
                a.wait_ge(hrow_dn, 2 * T)
                weights_hi(0, 0, (0, 1, 2), first=True)
                a.wait_ge(rt_ps, 1)
                a.activation(rt_cols, ps[4][0:NE, :], ACT.Exp, scale=-1.0).then_inc(rt_ex, 1)

                def x_out(e):
                    for j in range(2):
                        a.wait_ge(xt_ps, 2 * e + (1 + j))
                        a.activation(xeT_r[:, 4 * j:4 * j + 4, :],
                                     ps[2 + j][:, :].rearrange("p (k n) -> p k n", k=4), ACT.Copy).then_inc(xt_ev, 1)

                def silu(e, first=False):
                    a.wait_ge(gu_ps, 2 * e + 1)
                    if not first:
                        a.wait_ge(hid_dn, e)
                    a.activation(sg, ps[0][:, :], ACT.Silu).then_inc(sil, 1)

                def h_out(e):
                    a.wait_ge(ht_ps, e + 1)
                    a.activation(hT, ps[4][:, :].rearrange("p (k n) -> p k n", k=4), ACT.Copy).then_inc(ht_ev, 1)

                def expert_turn(e, odd, first=False):
                    silu(e, first)
                    weights_hi(e + 1, 1 - odd, (0, 1))
                    x_out(e + 1)
                    weights_hi(e + 1, 1 - odd, (2, 3))
                    h_out(e)

                a.wait_ge(tab_ps, 1)
                weights_hi(0, 0, (3,), first=True)
                x_out(0)
                expert_turn(0, 0, first=True)
                with a.Fori(0, NE // 2 - 1) as i:
                    expert_turn(2 * i + 1, 1)
                    expert_turn(2 * i + 2, 0)
                silu(NE - 1)
                x_out(NE)
                h_out(NE - 1)
                nov = a.value_load(ctl[0:1, 0:1], min_val=0, max_val=NOV)
                with a.Fori(0, NOV) as i:
                    with a.If(nov > i):
                        a.wait_ge(ov_xp, i + 1)
                        a.activation(xeT[:, 0:4, :], ps[2][:, :].rearrange("p (k n) -> p k n", k=4), ACT.Copy)
                        a.activation(xeT[:, 4:8, :], ps[3][:, :].rearrange("p (k n) -> p k n", k=4), ACT.Copy
                                     ).then_inc(ov_xe, 1)
                        a.wait_ge(ov_gu, i + 1)
                        a.activation(sg, ps[0][:, :], ACT.Silu).then_inc(ov_si, 1)
                        a.wait_ge(ov_hp, i + 1)
                        a.activation(hT, ps[4][:, :].rearrange("p (k n) -> p k n", k=4), ACT.Copy).then_inc(ov_he, 1)

            @block.vector
            def _(v):
                step = Counted(v, vch)

                def bc(ap, *shape):
                    return ap.to_broadcast([P, *shape])

                def ada_out(b):
                    n = group_no[("ada", b, 0)]
                    v.wait_ge(acc_ps, n + 1)
                    m_ = mod[:, 512 * b:512 * b + 512]
                    v.tensor_tensor(m_, ps[n % 2][:, :], m_, ALU.add).then_inc(ada_ev, 1)

                v.memset(prow[:], 0.0).then_inc(pads, 1)

                def w_out_add(t):
                    for b in range(2 if t < T else 0):
                        n = 2 * t + b
                        v.wait_ge(acc_ps, group_no[("out", b, t)] + 1)
                        x_ = x[:, t, 512 * b:512 * b + 512]
                        if n >= 2:
                            v.wait_ge(wo_ev, n - 1)
                        step(v.tensor_tensor(ws[:, n % 2, :], ps[group_no[("out", b, t)] % 2][:, :],
                                             mod[:, 2 * D + 512 * b:2 * D + 512 * b + 512], ALU.mult))
                        v.tensor_tensor(x_, x_, ws[:, n % 2, :], ALU.add).then_inc(wo_ev, 1)

                def h_low(t):
                    for j in range(2):
                        v.wait_ge(h_ev, 2 * t + j + 1)
                        v.tensor_tensor(hL[:, 4 * j:4 * j + 4, P * t:P * t + P],
                                        h_bank(0, t, j)[:, :].rearrange("p (k n) -> p k n", k=4),
                                        actT_r[:, 4 * j:4 * j + 4, P * t:P * t + P].bitcast(F32), ALU.subtract
                                        ).then_inc(hl_dn, 1)

                def in_weights_lo(i):
                    for half in range(2):
                        raw, lo, hi = in_part(IN_ORDER[i], half)
                        v.wait_ge(in_w_hi, 2 * i + half + 1)
                        v.tensor_tensor(lo, raw, hi.bitcast(F32), ALU.subtract).then_inc(in_w_lo, 1)

                def h_rows(base, shift, scale):
                    g_ = mod[:, D * scale:D * scale + D]
                    v.wait_ge(gain_ld, 16 + (16 if base else 0))
                    if base:
                        v.wait_ge(ada_ev, 7)
                    v.scalar_tensor_tensor(g_, g_, 1.0, gain[:], ALU.add, ALU.mult).then_inc(g_used, 1)
                    v.wait_ge(g_used, 2 if base else 1)
                    for t in range(T):
                        if base:
                            w_out_add(t + 1)
                        if base or t == 0:
                            v.wait_ge(xrs, t + 2 if base else 1)
                        h_ = h_row(base, t)
                        if t >= 2 and not base:
                            v.wait_ge(h_ps, 2 * (t - 1))
                        step(v.scalar_tensor_tensor(h_, x[:, t, :], rs_x[:, t:t + 1], g_, ALU.mult, ALU.mult))
                        v.tensor_tensor(h_, h_, mod[:, D * shift:D * shift + D], ALU.add).then_inc(hrow_dn, 1)
                        if not base and t:
                            h_low(t - 1)

                h_rows(0, 0, 1)
                h_low(T - 1)
                in_weights_lo(0)
                in_weights_lo(1)
                v.wait_ge(pcol_sb, 1)
                v.memset(xbcT[:, :, 0:3], 0.0).then_inc(pads, 1)
                v.wait_ge(pads, 2)
                for f in range(8):
                    v.wait_ge(win_ev, f + 1)
                    if f >= 2:
                        v.wait_ge(silu_dn, f - 1)
                    y_ = yt[:, f % 2, :]
                    step(v.tensor_scalar(y_, xbcT[:, f, 3:3 + S], pcol[:, 24 + f:25 + f], pcol[:, 32 + f:33 + f],
                                         ALU.mult, ALU.add))
                    for k in (2, 1, 0):
                        ins = v.scalar_tensor_tensor(y_, xbcT[:, f, k:k + S], pcol[:, 8 * k + f:8 * k + f + 1], y_,
                                                     ALU.mult, ALU.add)
                        if k:
                            step(ins)
                        else:
                            ins.then_inc(conv_dn, 1)
                    if f % 4 == 3:
                        in_weights_lo(2 + f // 4)
                in_weights_lo(4)
                in_weights_lo(5)
                v.wait_ge(par, 14 * 16)
                v.wait_ge(win_ev, 12)
                u3 = u.rearrange("p (t h) -> p t h", t=T)
                step(v.tensor_tensor(u3, proj[:, :, DT0:DT0 + NH], bc(hpar[:, 0:1, :], T, NH), ALU.add))
                v.scalar_tensor_tensor(au, u, -1.0, u, ALU.mult, ALU.max).then_inc(sp_u, 1)
                v.wait_ge(sp_e, 1)
                v.tensor_scalar(y1, ex, 1.0, None, ALU.add).then_inc(sp_y, 1)
                v.wait_ge(sp_y, 1)
                step(v.scalar_tensor_tensor(r1, y1, -1.0, ex, ALU.add, ALU.subtract))
                step(v.reciprocal(tend, y1))
                step(v.tensor_tensor(r1, r1, tend, ALU.mult))
                v.wait_ge(sp_l, 1)
                step(v.tensor_tensor(lny, lny, r1, ALU.subtract))
                step(v.scalar_tensor_tensor(dt, u, 0.0, lny, ALU.max, ALU.add))
                v.wait_ge(sp_e, 2)
                v.scalar_tensor_tensor(dta.rearrange("p (t h) -> p t h", t=T), dt.rearrange("p (t h) -> p t h", t=T),
                                       -1.0, bc(ealog.unsqueeze(1), T, NH), ALU.mult, ALU.mult).then_inc(dta_dn, 1)
                v.wait_ge(modb_ld, 16)
                ada_out(4)
                ada_out(5)
                v.wait_ge(crs, 2)
                step(v.tensor_tensor(proj[:, :, CQ0:CQ0 + 256], proj[:, :, CQ0:CQ0 + 256],
                                     bc(rs_c[:, 0:4].unsqueeze(2), T, 256), ALU.mult))
                v.tensor_tensor(proj[:, :, CKV0:CKV0 + 128], proj[:, :, CKV0:CKV0 + 128],
                                bc(rs_c[:, 4:8].unsqueeze(2), T, 128), ALU.mult).then_inc(c_nm, 1)
                v.wait_ge(cum_sb, 1)
                v.tensor_tensor(tend, tot, acs, ALU.subtract).then_inc(tend_d, 1)
                for j in range(3):
                    v.wait_ge(c_ps, j + 1)
                    v.tensor_scalar(cqT[:, j, :], ps[3 + j][:, :], pcol[:, 40 + j:41 + j], None, ALU.mult
                                    ).then_inc(c_ev, 1)
                v.wait_ge(cume, 3)
                for c in range(T):
                    b2 = c % 2
                    dtc = dt[:, 8 * c:8 * c + 8].unsqueeze(2)
                    x3 = xdt[:, b2, :].rearrange("p (h n) -> p h n", h=NH)
                    v.wait_ge(xs_cp, c + 1)
                    if c >= 2:
                        v.wait_ge(yd_ps, c - 1)
                        v.wait_ge(st_ps, c - 1)
                        v.wait_ge(y_dn, c - 1)
                        v.wait_ge(ysq, 2 * (c - 1))
                    step(v.tensor_tensor(x3, xs[:, b2, :].rearrange("p (h n) -> p h n", h=NH), bc(dtc, NH, HP), ALU.mult))
                    v.tensor_tensor(xde[:, b2, :].rearrange("p (h n) -> p h n", h=NH), x3,
                                    bc(tend[:, 8 * c:8 * c + 8].unsqueeze(2), NH, HP), ALU.mult).then_inc(xde_dn, 1)
                    for g in range(2):
                        v.wait_ge(dec_ps, 2 * c + g + 1)
                        if c > 0:
                            v.wait_ge(m_dn, 2 * c)
                        col = 8 * c + 4 * g
                        v.tensor_tensor(seg[:, g, :].rearrange("p (h l) -> p h l", h=4),
                                        ps[4 + g][:, :].rearrange("p (h l) -> p h l", h=4),
                                        bc(acs[:, col:col + 4].unsqueeze(2), 4, P), ALU.subtract).then_inc(seg_dn, 1)
                    v.wait_ge(bm_cp, c + 1)
                    for g in range(2):
                        v.wait_ge(seg_ex, 2 * c + g + 1)
                        if c > 0:
                            v.wait_ge(yd_ps, c)
                        cb = bmcb[:, b2, 256 + P * g:256 + P * g + P].unsqueeze(1)
                        v.tensor_tensor(mt[:, g, :].rearrange("p (h l) -> p h l", h=4),
                                        seg[:, g, :].rearrange("p (h l) -> p h l", h=4), bc(cb, 4, P), ALU.mult
                                        ).then_inc(m_dn, 1)
                    y_ = yt[:, b2, :]
                    y3 = y_.rearrange("p (h n) -> p h n", h=NH)
                    v.wait_ge(xd_dn, c + 1)
                    if c > 0:
                        v.wait_ge(yo_ps, c)
                        step(v.tensor_tensor(y3, ps[7][:, :].rearrange("p (h n) -> p h n", h=NH),
                                             bc(eac[:, 8 * c:8 * c + 8].unsqueeze(2), NH, HP), ALU.mult))
                        step(v.tensor_tensor(y_, y_, xd, ALU.add))
                        v.wait_ge(yd_ps, c + 1)
                        step(v.tensor_tensor(y_, ps[6][:, :], y_, ALU.add))
                    else:
                        v.wait_ge(yd_ps, 1)
                        step(v.tensor_tensor(y_, ps[6][:, :], xd, ALU.add))
                    v.tensor_tensor(proj[:, c, 0:512], y_, proj[:, c, 0:512], ALU.mult).then_inc(y_dn, 1)
                    if c < T - 1:
                        v.wait_ge(st_ps, c + 1)
                        if c == 0:
                            v.tensor_copy(hst, ps[0][:, :]).then_inc(h_dn, 1)
                        else:
                            h3 = hst.rearrange("p (h n) -> p h n", h=NH)
                            v.wait_ge(yo_ps, c)
                            step(v.tensor_tensor(h3, h3, bc(cd[:, 8 * c:8 * c + 8].unsqueeze(2), NH, HP), ALU.mult))
                            v.tensor_tensor(hst, hst, ps[0][:, :], ALU.add).then_inc(h_dn, 1)
                v.wait_ge(y_dn, 4)
                v.wait_ge(yrs, 1)
                for c in range(T):
                    for g in range(2):
                        y_ = proj[:, c, 256 * g:256 * g + 256]
                        step(v.tensor_scalar(y_, y_, rs_y[:, 2 * c + g:2 * c + g + 1], None, ALU.mult))
                ada_out(6)

                def squares(src, width, col):
                    s_ = sq[:, 0:T * width]
                    step(v.tensor_tensor(s_.rearrange("p (t n) -> p t n", t=T), src, src, ALU.mult))
                    step(v.tensor_reduce(ss_h[:, col:col + 16], s_.rearrange("p (a n) -> p a n", a=16), AX.X, ALU.add))

                v.wait_ge(y_dn, 4)
                v.wait_ge(ysq, 8)
                squares(proj[:, :, MQ0:MQ0 + 256], 256, 32)
                squares(proj[:, :, MK0:MK0 + 256], 256, 48)
                ada_out(7)
                v.wait_ge(qkv_ev, 2 * T)
                kno = kv.rearrange("p t (h n) -> p t h n", h=MH)[:, :, :, 0:DN]
                sq3 = sq[:, 0:T * 256].rearrange("p (t h n) -> p t h n", t=T, h=MH)
                step(v.tensor_tensor(sq3, kno, kno, ALU.mult))
                step(v.tensor_reduce(ss_h[:, 16:32], sq[:, 0:T * 256].rearrange("p (a n) -> p a n", a=16), AX.X, ALU.add))
                ada_out(8)
                v.wait_ge(kr_dn, 1)
                squares(qrow, 384, 0)
                kr = proj[:, :, KR0:KR0 + DR]
                sq4 = sq[:, 0:T * DR].rearrange("p (t n) -> p t n", t=T)
                step(v.tensor_tensor(sq4, kr, kr, ALU.mult))
                step(v.tensor_reduce(ss_kr, sq4, AX.X, ALU.add))
                ssk = ss_h[:, 16:32].rearrange("p (t h) -> p t h", t=T)
                v.tensor_tensor(ssk, ssk, bc(ss_kr.unsqueeze(2), T, MH), ALU.add).then_inc(hss, 1)
                ada_out(9)
                v.wait_ge(hrs, 1)

                def out_weights_lo(b, half):
                    v.wait_ge(out_w_hi, 2 * b + half + 1)
                    raw, lo, hi = out_part(b, half)
                    v.tensor_tensor(lo, raw, hi.bitcast(F32), ALU.subtract).then_inc(out_w_lo, 1)

                def stage(h):
                    if h >= 2:
                        v.wait_ge(qk_ps, h - 1)
                    q3 = qn[:, h % 2, :].rearrange("p (t n) -> p t n", t=T)
                    k3 = kn[:, h % 2, :].rearrange("p (t n) -> p t n", t=T)
                    hh = h % MH
                    c0 = 0 if h < MH else 32
                    rq = rs_h[:, c0:c0 + 16].rearrange("p (t h) -> p t h", t=T)[:, :, hh:hh + 1]
                    rk_ = rs_h[:, c0 + 16:c0 + 32].rearrange("p (t h) -> p t h", t=T)[:, :, hh:hh + 1]
                    if h < MH:
                        step(v.tensor_tensor(q3, qrow[:, :, DQ * hh:DQ * hh + DQ], bc(rq, T, DQ), ALU.mult))
                        step(v.tensor_tensor(k3[:, :, 0:DN], kv[:, :, 128 * hh:128 * hh + DN], bc(rk_, T, DN), ALU.mult))
                        v.tensor_tensor(k3[:, :, DN:DQ], kr, bc(rk_, T, DR), ALU.mult).then_inc(stg, 1)
                    else:
                        step(v.tensor_tensor(q3[:, :, 0:HP], proj[:, :, MQ0 + HP * hh:MQ0 + HP * hh + HP],
                                             bc(rq, T, HP), ALU.mult))
                        v.tensor_tensor(k3[:, :, 0:HP], proj[:, :, MK0 + HP * hh:MK0 + HP * hh + HP],
                                        bc(rk_, T, HP), ALU.mult).then_inc(stg, 1)

                def q_out(h):
                    d = DQK[h]
                    v.wait_ge(qk_ps, h + 1)
                    if h >= 2:
                        v.wait_ge(s_ps, T * (h - 1))
                    v.tensor_scalar(qT[0:d, h % 2, :], ps[0][0:d, :],
                                    pcol[0:d, (51 if h < MH else 53):(52 if h < MH else 54)], float(d) ** -0.5,
                                    ALU.mult, ALU.mult).then_inc(q_sb, 1)

                def biased(n):
                    h, t = n // T, n % T
                    w = P * (t + 1)
                    v.wait_ge(s_ps, n + 1)
                    if n >= 2:
                        v.wait_ge(p_dn, n - 1)
                    b_ = cst[:, C_MASK + S - w:C_MASK + S] if h < MH else biasm[:, h - MH, S - w:S]
                    if n == MH * T:
                        v.wait_ge(bias_ld, 16)
                    v.tensor_tensor_reduce(ssb[:, n % 2, 0:w], ps[2 + n % 2][:, 0:w], b_, -1.0, 3.0e38,
                                           ALU.add, ALU.min, mx[:, n % 8:n % 8 + 1]).then_inc(s_sb, 1)

                def head_out(h):
                    v.wait_ge(pv_ps, T * (h + 1))
                    step(v.reciprocal(linv, lsum[:, 4 * (h % 2):4 * (h % 2) + 4]))
                    v.tensor_tensor(proj[:, :, o_col[h]:o_col[h] + DV],
                                    ps[6 + h % 2][:, 0:256].rearrange("p (t n) -> p t n", t=T),
                                    bc(linv.unsqueeze(2), T, DV), ALU.mult).then_inc(o_dn, 1)

                stage(0)
                q_out(0)
                stage(1)
                for n in range(8 * T):
                    h, t = n // T, n % T
                    biased(n)
                    if t == 0 and h + 1 < 8:
                        q_out(h + 1)
                    if t == 1 and h + 2 < 8:
                        stage(h + 2)
                    if t == 2 and h > 0:
                        head_out(h - 1)
                    if n in (26, 30):
                        out_weights_lo(0, (n - 26) // 4)
                head_out(7)
                ada_out(10)
                v.wait_ge(yrs, 2)
                v.wait_ge(o_dn, 8)
                step(v.tensor_tensor(proj[:, :, CQ0:CQ0 + 256], proj[:, :, CQ0:CQ0 + 256],
                                     bc(rs_y[:, 8:12].unsqueeze(2), T, 256), ALU.mult))
                v.tensor_tensor(proj[:, :, MQ0:MQ0 + 256], proj[:, :, MQ0:MQ0 + 256],
                                bc(rs_y[:, 12:16].unsqueeze(2), T, 256), ALU.mult).then_inc(yn, 1)
                for j in range(KD):
                    v.wait_ge(yc_hi, j + 1)
                    v.scalar_tensor_tensor(yL[:, j, :], ps[2 + j % 4][:, :], pcol[:, 43 + j:44 + j],
                                           actT_r[:, j, :].bitcast(F32), ALU.mult, ALU.subtract).then_inc(yc_ev, 1)
                out_weights_lo(1, 0)
                out_weights_lo(1, 1)
                w_out_add(0)
                h_rows(T, 3, 4)

                def weights_lo(e, odd, parts):
                    for m in parts:
                        j, k0, k1, buf = hi_parts[m]
                        v.wait_ge(w_hi, 4 * e + (m + 1))
                        v.tensor_tensor(slots_r[3 * odd + j][:, 512 * k0:512 * k1],
                                        slots[3 * odd + j][:, 512 * k0:512 * k1], buf.bitcast(F32), ALU.subtract
                                        ).then_inc(w_lo, 1)

                weights_lo(0, 0, (0, 1, 2))
                def r3(ap, a_):
                    return ap.rearrange("p (a b) -> p a b", a=a_)

                v.wait_ge(rt_rows, 1)
                step(v.tensor_scalar(sc, ps[5][:, 0:T * NE], 1.0, None, ALU.add))
                step(v.reciprocal(sc, sc))
                step(v.tensor_tensor(r3(bi, T), r3(sc, T), bc(rbias[:].unsqueeze(1), T, NE), ALU.add))
                b3 = r3(bi, 16)
                hi2, lo2 = r3(mm2[:, 0:32], 16), r3(mm2[:, 32:64], 16)
                step(v.tensor_tensor(hi2, b3[:, :, 0:2], b3[:, :, 2:4], ALU.max))
                step(v.tensor_tensor(lo2, b3[:, :, 0:2], b3[:, :, 2:4], ALU.min))
                g1, g2, g3 = gs.unsqueeze(2), gw.unsqueeze(2), gsel.unsqueeze(2)
                step(v.tensor_tensor(g1, hi2[:, :, 0:1], hi2[:, :, 1:2], ALU.max))
                step(v.tensor_tensor(g2, hi2[:, :, 0:1], hi2[:, :, 1:2], ALU.min))
                step(v.tensor_tensor(g3, lo2[:, :, 0:1], lo2[:, :, 1:2], ALU.max))
                step(v.tensor_tensor(gw, gw, gsel, ALU.max))
                step(v.tensor_tensor(gs, gs, gw, ALU.add))

                def first_max(dst, src, n, rev, tmp):
                    r_ = red[:, 0:4]
                    s3, t3, d3 = r3(src, T), r3(tmp, T), r3(dst, T)
                    step(v.tensor_reduce(r_, s3, AX.X, ALU.max))
                    step(v.tensor_tensor(t3, s3, bc(r_.unsqueeze(2), T, n), ALU.is_equal))
                    step(v.tensor_tensor(t3, t3, bc(cst[:, rev:rev + n].unsqueeze(1), T, n), ALU.mult))
                    step(v.tensor_reduce(r_, t3, AX.X, ALU.max))
                    step(v.tensor_tensor(d3, t3, bc(r_.unsqueeze(2), T, n), ALU.is_equal))

                first_max(gsel, gs, 4, C_REV4, gw)
                step(v.tensor_scalar(gw, gsel, -NEG, NEG, ALU.mult, ALU.add))
                step(v.tensor_tensor(r3(mb, 16), b3, bc(gsel.unsqueeze(2), 16, 4), ALU.mult))
                step(v.tensor_tensor(r3(mb, 16), r3(mb, 16), bc(gw.unsqueeze(2), 16, 4), ALU.add))
                first_max(oh1, mb, NE, C_REV16, eqw)
                step(v.scalar_tensor_tensor(mb, oh1, 100 * NEG, mb, ALU.mult, ALU.add))
                first_max(oh2, mb, NE, C_REV16, eqw)
                v.tensor_tensor(both, oh1, oh2, ALU.add).then_inc(both_dn, 1)
                ada_out(11)


                def of_choice(dst, src):
                    step(v.tensor_tensor(oh_v, oh12, bc(src.unsqueeze(1), 2, T * NE), ALU.mult))
                    return v.tensor_reduce(dst.rearrange("p a t -> p (a t)"),
                                           oh_v.rearrange("p a (t e) -> p (a t) e", t=T), AX.X, ALU.add)

                step(of_choice(w12, sc))
                step(v.tensor_tensor(wsum, w12[:, 0, :], w12[:, 1, :], ALU.add))
                step(v.reciprocal(wsum, wsum))
                step(v.tensor_tensor(w12, w12, bc(wsum.unsqueeze(1), 2, T), ALU.mult))
                v.wait_ge(rk_ps, 1)
                c_, o_ = ps[6][0:NE, 0:1], ov[0:NE, :]
                step(v.tensor_scalar(o_, c_, float(P), None, ALU.is_gt))
                step(v.scalar_tensor_tensor(o_, c_, float(2 * P), o_, ALU.is_gt, ALU.add))
                v.scalar_tensor_tensor(o_, c_, float(3 * P), o_, ALU.is_gt, ALU.add).then_inc(ov_dn, 1)
                step(v.tensor_copy(tmpr, ps[5][:, 0:64]))
                step(v.tensor_scalar(jt, tmpr, float(P), None, ALU.is_ge))
                step(v.tensor_copy(tmps, jt))
                step(v.scalar_tensor_tensor(jt, tmpr, float(2 * P), jt, ALU.is_ge, ALU.add))
                step(v.scalar_tensor_tensor(jt, tmpr, float(3 * P), jt, ALU.is_ge, ALU.add))
                step(v.scalar_tensor_tensor(rowf, jt, float(-P), tmpr, ALU.mult, ALU.add))
                step(of_choice(rf, rowf))
                step(v.tensor_tensor(r3(tilef, T), r3(jt, T), bc(cst[:, C_IOTA16:C_IOTA16 + NE].unsqueeze(1), T, NE),
                                     ALU.add))
                v.wait_ge(ovb_ps, 1)
                step(v.tensor_copy(ovb, ps[7][:, 0:33]))
                step(v.scalar_tensor_tensor(c1, ovb[:, 0:16], float(NE - 1), cst[:, C_IOTA16:C_IOTA16 + NE],
                                            ALU.add, ALU.subtract))
                step(v.tensor_tensor(r3(tmps, T), r3(tmps, T), bc(c1.unsqueeze(1), T, NE), ALU.mult))
                step(v.tensor_tensor(tilef, tilef, tmps, ALU.add))
                step(of_choice(tf, tilef))
                for j in range(2):
                    for t in range(T):
                        m = T * j + t
                        v.tensor_scalar(row_oh[:, m, :], cst[:, C_IOTA:C_IOTA + P], rf[:, j, t:t + 1], None, ALU.is_equal)
                        v.tensor_scalar(tile_tok[:, m, :], cst[:, C_IOTA:C_IOTA + NT], tf[:, j, t:t + 1],
                                        cst[:, C_TOK + t:C_TOK + t + 1], ALU.is_equal, ALU.mult).then_inc(sel_dn, 1)
                step(v.scalar_tensor_tensor(pf, rf, float(NT), tf, ALU.mult, ALU.add))
                v.tensor_copy(pos_i[:], pf).then_inc(pos_dn, 1)
                v.wait_ge(tab_ps, 1)
                v.tensor_copy(slot_idx[:], ps[3][:, 0:NT]).then_inc(tab_sb, 1)
                e7 = r3(cmp7[0:1, :], NOV)
                step(v.tensor_tensor(e7, ovb[0:1, 17:33].unsqueeze(1).to_broadcast([1, NOV, NE]),
                                     cst[0:1, C_IOTA7:C_IOTA7 + NOV].unsqueeze(2).to_broadcast([1, NOV, NE]), ALU.is_le))
                step(v.tensor_reduce(ctf[0:1, 1:8], e7, AX.X, ALU.add))
                step(v.tensor_copy(ctf[0:1, 0:1], ovb[0:1, 16:17]))
                v.tensor_copy(ctl[:], ctf[0:1, 0:8]).then_inc(pos_dn, 1)

                gf = mod[:, 5 * D:6 * D]

                def hidden(e, first=False):
                    v.wait_ge(sil, e + 1)
                    v.wait_ge(gu_ps, 2 * e + 2)
                    if not first:
                        v.wait_ge(ht_ps, e)
                    v.tensor_tensor(hid, ps[1][:, :], sg, ALU.mult).then_inc(hid_dn, 1)

                def y_out(e, odd, first=False):
                    if not first:
                        v.wait_ge(yw[odd], 8 * (e - 1) if odd else 8 * e)
                    for b in range(2):
                        v.wait_ge(y_ps, 2 * e + (1 + b))
                        v.tensor_tensor(ysb[:, odd, 512 * b:512 * b + 512], ps[6 + b][:, :],
                                        gf[:, 512 * b:512 * b + 512], ALU.mult).then_inc(y_ev, 1)

                def x_low(e):
                    for j in range(2):
                        v.wait_ge(xt_ev, 2 * e + (1 + j))
                        v.tensor_tensor(xeL[:, 4 * j:4 * j + 4, :], ps[2 + j][:, :].rearrange("p (k n) -> p k n", k=4),
                                        xeT_r[:, 4 * j:4 * j + 4, :].bitcast(F32),
                                        ALU.subtract).then_inc(xl_dn, 1)


                def expert_turn(e, odd, first=False):
                    weights_lo(e + 1, 1 - odd, (0, 1))
                    hidden(e, first)
                    x_low(e + 1)
                    weights_lo(e + 1, 1 - odd, (2, 3))

                x_low(0)
                weights_lo(0, 0, (3,))
                expert_turn(0, 0, first=True)
                expert_turn(1, 1)
                y_out(0, 0, first=True)
                expert_turn(2, 0)
                y_out(1, 1, first=True)
                expert_turn(3, 1)
                y_out(2, 0)
                with v.Fori(0, NE // 2 - 3) as i:
                    expert_turn(2 * i + 4, 0)
                    y_out(2 * i + 3, 1)
                    expert_turn(2 * i + 5, 1)
                    y_out(2 * i + 4, 0)
                expert_turn(NE - 2, 0)
                y_out(NE - 3, 1)
                hidden(NE - 1)
                y_out(NE - 2, 0)
                y_out(NE - 1, 1)
                v.wait_ge(y_ev, 2 * NE)
                v.wait_ge(pos_dn, 2)
                nov = v.value_load(ctl[0:1, 0:1], min_val=0, max_val=NOV)
                with v.Fori(0, NOV) as i:
                    with v.If(nov > i):
                        v.wait_ge(ov_si, i + 1)
                        v.tensor_tensor(hid, ps[1][:, :], sg, ALU.mult).then_inc(ov_hd, 1)
                        v.wait_ge(ov_yp, i + 1)
                        v.tensor_tensor(ysb[:, 0, 0:512], ps[6][:, :], gf[:, 0:512], ALU.mult)
                        v.tensor_tensor(ysb[:, 0, 512:1024], ps[7][:, :], gf[:, 512:1024], ALU.mult).then_inc(ov_ye, 1)
                for t in range(T):
                    v.wait_ge(cg[t], 32)
                    step(v.scalar_tensor_tensor(x[:, t, :], chosen[:, 2 * t, :], w12[:, 0, t:t + 1], x[:, t, :],
                                                ALU.mult, ALU.add))
                    v.scalar_tensor_tensor(x[:, t, :], chosen[:, 2 * t + 1, :], w12[:, 1, t:t + 1], x[:, t, :],
                                           ALU.mult, ALU.add).then_inc(cdn, 1)
                with v.If(L < DEPTH - 1):
                    first_ada_out(v, (5, 0, 1, 2))

            @block.gpsimd
            def _(g):
                step = Counted(g, gch)

                def rstd(dst, src, width, done):
                    step(g.tensor_scalar(dst, src, 1.0 / width, EPS, ALU.mult, ALU.add))
                    g.tensor_tensor(dst, dst, cst[:, C_HALF:C_HALF + 1].to_broadcast(list(dst.shape)), ALU.pow
                                    ).then_inc(done, 1)

                g.wait_ge(xss, T)
                rstd(rs_x, ss_x, D, xrs)
                g.wait_ge(h_ps, 2 * T)
                step(g.memset(zeros, 0.0))
                y3_ = y_rows.rearrange("(p n) d -> p n d", n=NT)[:, NE:NT, :].rearrange("p n (b m) -> p (n b) m", b=2)
                g.dma_start(y3_, zeros.unsqueeze(1).to_broadcast([P, 2 * (NT - NE), 512])).then_inc(zero_wr, 16)
                g.wait_ge(c_ss, 2 * T)
                rstd(rs_c[:, 0:4], ss_c[:, 0:4], 256, crs)
                rstd(rs_c[:, 4:8], ss_c[:, 4:8], 128, crs)
                for c in range(T):
                    g.wait_ge(xs_cp, c + 1)
                    if c > 0:
                        g.wait_ge(y_dn, c)
                    else:
                        g.wait_ge(h_ps, 2 * T)
                        g.wait_ge(par, 14 * 16)
                    g.tensor_tensor(xd.rearrange("p (h n) -> p h n", h=NH), xs[:, c % 2, :].rearrange("p (h n) -> p h n", h=NH),
                                    hpar[:, 2, :].unsqueeze(2).to_broadcast([P, NH, HP]), ALU.mult).then_inc(xd_dn, 1)
                g.wait_ge(ysq, 8)
                rstd(rs_y[:, 0:8], ss_y[:, 0:8], 256, yrs)
                cos = cst[:, C_COS:C_COS + 64].rearrange("p (t n) -> p t n", t=T)
                sin = cst[:, C_SIN:C_SIN + 64].rearrange("p (t n) -> p t n", t=T)
                g.wait_ge(y_dn, 4)
                g.wait_ge(qkv_ev, 2 * T)
                for h in range(MH + 1):
                    src = qrow[:, :, DQ * h + DN:DQ * h + DQ] if h < MH else proj[:, :, KR0:KR0 + DR]
                    x1, x2 = src[:, :, 0:16], src[:, :, 16:32]
                    ta, tb, tc, td = (rtmp[:, k, 64 * h:64 * h + 64].rearrange("p (t n) -> p t n", t=T) for k in range(4))
                    g.tensor_tensor(ta, x1, cos, ALU.mult).then_inc(gch, 1)
                    g.tensor_tensor(tb, x2, sin, ALU.mult).then_inc(gch, 1)
                    g.tensor_tensor(tc, x1, sin, ALU.mult).then_inc(gch, 1)
                    g.tensor_tensor(td, x2, cos, ALU.mult).then_inc(gch, 1)
                    step.n += 4
                    g.wait_ge(gch, step.n)
                    step(g.tensor_tensor(x1, ta, tb, ALU.subtract))
                    ins = g.tensor_tensor(x2, tc, td, ALU.add)
                    if h < MH:
                        step(ins)
                    else:
                        ins.then_inc(kr_dn, 1)
                g.wait_ge(yss, 2 * T)
                rstd(rs_y[:, 8:16], ss_y[:, 8:16], 256, yrs)
                hf = hf_rows.rearrange("(t p) d -> t p d", p=P)
                for t in range(T):
                    g.wait_ge(xss, T + t + 1)
                    rstd(rs_x[:, t:t + 1], ss_x[:, t:t + 1], D, xrs)
                    g.wait_ge(hrow_dn, T + t + 1)
                    g.dma_start(hf[t], h_row(T, t)).then_inc(hf_wr, 16)
                g.wait_ge(hf_wr, 16 * T)
                g.wait_ge(zero_wr, 16)
                g.wait_ge(tab_sb, 1)

                def gather(dst, col, sem_):
                    g.indirect_dma_start(out=dst, out_offset=None, in_=hf_rows,
                                         in_offset=bass.IndirectOffsetOnAxis(ap=col, axis=0)).then_inc(sem_, 16)

                yv = y_rows.rearrange("(p n) d -> n p d", n=NT)

                for e in range(NE + 4):
                    if e <= NE:
                        if e >= 2:
                            g.wait_ge(xt_ps, 2 * e - 2)
                        gather(xg[:, e % 2, :], slot_idx[:, e:e + 1], gat[e % 2])
                    if e >= 4:
                        g.wait_ge(y_ev, 2 * (e - 4) + 2)
                        g.dma_start(yv[e - 4], ysb[:, e % 2, :]).then_inc(yw[e % 2], 16)
                g.wait_ge(yw[0], 16 * NE // 2)
                g.wait_ge(yw[1], 16 * NE // 2)
                g.wait_ge(pos_dn, 2)
                g.wait_ge(xt_ev, 2 * NE + 2)
                g.memset(turn_mark[:], 0).then_inc(turn, 1)
                nov = g.value_load(ctl[0:1, 0:1], min_val=0, max_val=NOV)
                for i in range(NOV):
                    with g.If(nov > i):
                        gather(xg[:, 1, :], slot_idx[:, NE + i:NE + i + 1], ov_g)
                        g.wait_ge(ov_ye, i + 1)
                        g.dma_start(yv[NE + i], ysb[:, 0, :]).then_inc(ov_yw, 16)
                        g.wait_ge(ov_yw, 16 * i + 16)
                        g.memset(turn_mark[:], 0).then_inc(turn, 1)
                for t in range(T):
                    for j in range(2):
                        g.indirect_dma_start(out=chosen[:, 2 * t + j, :], out_offset=None, in_=y_rows,
                                             in_offset=bass.IndirectOffsetOnAxis(ap=pos_i[:, j, t:t + 1], axis=0)
                                             ).then_inc(cg[t], 16)
                for t in range(T):
                    g.wait_ge(cg[t], 32)
                g.dma_reset(range(first, last + 1))
        nc.all_engine_barrier(sems_to_clear=range(first, last + 1))

    with nc.Block() as block:
        @block.sync
        def _(sp):
            sp.dma_start(out.rearrange("a (t p) d -> p (a t) d", p=P), x[:]).then_inc(par, 16)
            sp.wait_ge(par, 16)
    ctx.close()


_INS = ["x", "c", "ada_w", "ada_b", "norm_mix_g", "norm_ffn_g", "w_in", "ssd_conv_w", "ssd_conv_b", "ssd_dt_bias",
        "ssd_a_log", "ssd_d", "ssd_norm_g", "mla_q_norm_g", "mla_w_uq", "mla_kv_norm_g", "mla_w_ukv", "mla_q_gain",
        "mla_k_gain", "mla_out_g", "moba_q_gain", "moba_k_gain", "moba_out_g", "rel_bias", "w_out", "router_w",
        "router_bias", "moe_w_gate", "moe_w_up", "moe_w_down"]


def kernel(**inputs):
    import concourse.bacc as _bacc
    from concourse.bass_utils import run_bass_kernel_spmd as _run

    nc = _bacc.Bacc("TRN2", target_bir_lowering=False, num_devices=1)
    arrays, aps = {}, {}
    for name in _INS:
        a = np.ascontiguousarray(inputs[name])
        arrays[f"in_{name}"] = a
        aps[name] = nc.dram_tensor(f"in_{name}", a.shape, mybir.dt.from_np(a.dtype), kind="ExternalInput").ap()
    cpack, bucket_oh = shape_constants()
    arrays["shape_constants"], arrays["bucket_one_hot"] = cpack, bucket_oh
    cp = nc.dram_tensor("shape_constants", cpack.shape, F32, kind="ExternalInput").ap()
    bo = nc.dram_tensor("bucket_one_hot", bucket_oh.shape, F32, kind="ExternalInput").ap()
    out = nc.dram_tensor("out", (1, S, D), F32, kind="ExternalOutput").ap()
    relv = nc.dram_tensor("bias_by_distance", (MH, P, 640), F32, kind="Internal").ap()
    hf_rows = nc.dram_tensor("ffn_rows", (S, D), F32, kind="Internal").ap()
    y_rows = nc.dram_tensor("expert_rows", (P * NT, D), F32, kind="Internal").ap()
    trunk(nc, aps, out, cp, bo, relv, hf_rows, y_rows)
    r = _run(nc, [arrays], core_ids=[0])
    return r.results[0]["out"]
```
